# Optimizing a Trainium2 kernel written in Bass

```python
import jax, jax.numpy as jnp
from jax import lax
import numpy as np
import math

D_MODEL = 1024
BATCH = 1
SEQ = 256
DEPTH = 2

POOL_WINDOWS = (2, 4, 8, 16)
POOL_GROUP = 128
POOL_WIDTH = POOL_GROUP * len(POOL_WINDOWS)
ATTN_HEADS = 8
HEAD_DIM = 64
ATTN_WIDTH = ATTN_HEADS * HEAD_DIM
MOBA_BLOCK = 256
MOBA_TOPK = 3
Q_CHUNK = 64
RNN_BLOCKS = 10
RNN_BLOCK = 128
RNN_WIDTH = RNN_BLOCKS * RNN_BLOCK
RNN_CONV = 4
RG_C = 8.0
D_FF = 2816
FFN_CONV = 3
EPS = 1e-6
NEG_INF = -1e30
N_EVEN = (DEPTH + 1) // 2
N_ODD = DEPTH // 2


def rms_norm(x, g):
    x32 = x.astype(jnp.float32)
    y = x32 * lax.rsqrt(jnp.mean(x32 * x32, axis=-1, keepdims=True) + EPS)
    return (y * g.astype(jnp.float32)).astype(x.dtype)

def causal_dwconv(x, w, b):
    K, C = w.shape
    y = lax.conv_general_dilated(
        x, w[:, None, :].astype(x.dtype), window_strides=(1,), padding=[(K - 1, 0)],
        dimension_numbers=('NWC', 'WIO', 'NWC'), feature_group_count=C)
    return y + b.astype(x.dtype)

def multiscale_pool_minus_identity(u):
    S = u.shape[1]
    u32 = u.astype(jnp.float32)
    cs = jnp.cumsum(u32, axis=1)
    count = jnp.arange(1, S + 1, dtype=jnp.float32)[None, :, None]
    outs = []
    for gi, w in enumerate(POOL_WINDOWS):
        sl = slice(gi * POOL_GROUP, (gi + 1) * POOL_GROUP)
        c = cs[..., sl]
        prev = jnp.pad(c, ((0, 0), (w, 0), (0, 0)))[:, :S]
        outs.append((c - prev) / jnp.minimum(count, float(w)) - u32[..., sl])
    return jnp.concatenate(outs, axis=-1)

def head_rms(t, g):
    t32 = t.astype(jnp.float32)
    return t32 * lax.rsqrt(jnp.mean(t32 * t32, axis=-1, keepdims=True) + EPS) * g.astype(jnp.float32)

def moba_attention(q, k, v, q_gain, k_gain):
    B, S, H, Dh = q.shape
    nb = -(-S // MOBA_BLOCK)
    s_pad = nb * MOBA_BLOCK
    pad = ((0, 0), (0, s_pad - S), (0, 0), (0, 0))
    qn = jnp.pad(head_rms(q, q_gain), pad).transpose(0, 2, 1, 3)
    kn = jnp.pad(head_rms(k, k_gain), pad).transpose(0, 2, 1, 3)
    vp = jnp.pad(v.astype(jnp.float32), pad).transpose(0, 2, 1, 3)
    k_blocks = kn.reshape(B, H, nb, MOBA_BLOCK, Dh)
    v_blocks = vp.reshape(B, H, nb, MOBA_BLOCK, Dh)
    slopes = 2.0 ** (-8.0 * jnp.arange(1, H + 1, dtype=jnp.float32) / H)
    scale = Dh ** -0.5
    topk = min(MOBA_TOPK, nb - 1)
    q_blk = jnp.arange(s_pad) // MOBA_BLOCK
    if topk > 0:
        k_mean = jnp.mean(k_blocks, axis=3)
        gate = jnp.einsum('bhqd,bhnd->bhqn', qn, k_mean)
        past = jnp.arange(nb)[None, :] < q_blk[:, None]
        gate = jnp.where(past[None, None], gate, -jnp.inf)
        _, sel_idx = lax.top_k(gate, topk)
        sel_valid = sel_idx < q_blk[None, None, :, None]
    bi = jnp.arange(B)[:, None, None, None]
    hi = jnp.arange(H)[None, :, None, None]
    kpos = jnp.arange(MOBA_BLOCK)

    def chunk(c):
        start = c * Q_CHUNK
        q_c = lax.dynamic_slice_in_dim(qn, start, Q_CHUNK, axis=2)
        t_c = start + jnp.arange(Q_CHUNK)
        own = start // MOBA_BLOCK
        k_own = lax.dynamic_index_in_dim(k_blocks, own, axis=2, keepdims=False)
        v_own = lax.dynamic_index_in_dim(v_blocks, own, axis=2, keepdims=False)
        dist_own = (t_c[:, None] - (own * MOBA_BLOCK + kpos)[None, :]).astype(jnp.float32)
        logit_own = (jnp.einsum('bhqd,bhkd->bhqk', q_c, k_own) * scale
                     - slopes[None, :, None, None] * dist_own[None, None])
        logit_own = jnp.where((dist_own >= 0)[None, None], logit_own, NEG_INF)
        if topk == 0:
            p_own = jax.nn.softmax(logit_own, axis=-1)
            return jnp.einsum('bhqk,bhkd->bhqd', p_own, v_own)
        idx_c = lax.dynamic_slice_in_dim(sel_idx, start, Q_CHUNK, axis=2)
        valid_c = lax.dynamic_slice_in_dim(sel_valid, start, Q_CHUNK, axis=2)
        k_sel = k_blocks[bi, hi, idx_c]
        v_sel = v_blocks[bi, hi, idx_c]
        s_pos = idx_c[..., None] * MOBA_BLOCK + kpos
        dist_sel = (t_c[None, None, :, None, None] - s_pos).astype(jnp.float32)
        logit_sel = (jnp.einsum('bhqd,bhqjkd->bhqjk', q_c, k_sel) * scale
                     - slopes[None, :, None, None, None] * dist_sel)
        logit_sel = jnp.where(valid_c[..., None], logit_sel, NEG_INF)
        n_sel = topk * MOBA_BLOCK
        logits = jnp.concatenate([logit_sel.reshape(B, H, Q_CHUNK, n_sel), logit_own], axis=-1)
        p = jax.nn.softmax(logits, axis=-1)
        p_sel = p[..., :n_sel].reshape(B, H, Q_CHUNK, topk, MOBA_BLOCK)
        p_own = p[..., n_sel:]
        return (jnp.einsum('bhqjk,bhqjkd->bhqd', p_sel, v_sel)
                + jnp.einsum('bhqk,bhkd->bhqd', p_own, v_own))

    outs = lax.map(chunk, jnp.arange(s_pad // Q_CHUNK))
    out = outs.transpose(1, 0, 3, 2, 4).reshape(B, s_pad, H * Dh)
    return out[:, :S]

def pool_attn_mixer(h, w_in, pool_w, pool_scale, q_gain, k_gain, w_out):
    B, S, _ = h.shape
    z = h @ w_in
    u, q, k, v = jnp.split(z, [POOL_WIDTH, POOL_WIDTH + ATTN_WIDTH, POOL_WIDTH + 2 * ATTN_WIDTH], axis=-1)
    p = multiscale_pool_minus_identity(u).astype(h.dtype)
    p = jnp.einsum('bsgc,gcd->bsgd', p.reshape(B, S, len(POOL_WINDOWS), POOL_GROUP), pool_w)
    p = p.reshape(B, S, POOL_WIDTH) * pool_scale
    a = moba_attention(q.reshape(B, S, ATTN_HEADS, HEAD_DIM), k.reshape(B, S, ATTN_HEADS, HEAD_DIM),
                       v.reshape(B, S, ATTN_HEADS, HEAD_DIM), q_gain, k_gain)
    return jnp.concatenate([p, a.astype(h.dtype)], axis=-1) @ w_out

def rglru_mixer(h, w_in, conv_w, conv_b, w_a, b_a, w_x, b_x, lam, w_out):
    B, S, _ = h.shape
    z = h @ w_in
    gate, xr = jnp.split(z, 2, axis=-1)
    xr = causal_dwconv(xr, conv_w, conv_b)
    xb = xr.reshape(B, S, RNN_BLOCKS, RNN_BLOCK)
    r = jax.nn.sigmoid((jnp.einsum('bsnc,ncd->bsnd', xb, w_a).reshape(B, S, RNN_WIDTH) + b_a).astype(jnp.float32))
    i = jax.nn.sigmoid((jnp.einsum('bsnc,ncd->bsnd', xb, w_x).reshape(B, S, RNN_WIDTH) + b_x).astype(jnp.float32))
    log_a = -RG_C * r * jax.nn.softplus(-lam.astype(jnp.float32))
    a = jnp.exp(log_a)
    b = jnp.sqrt(-jnp.expm1(2.0 * log_a)) * (i * xr.astype(jnp.float32))

    def combine(left, right):
        a1, b1 = left
        a2, b2 = right
        return a1 * a2, a2 * b1 + b2

    _, hs = lax.associative_scan(combine, (a, b), axis=1)
    y = jax.nn.gelu(gate) * hs.astype(gate.dtype)
    return y @ w_out

def conv_ffn(h, w_in, conv_w, conv_b, w_out):
    z = causal_dwconv(h @ w_in, conv_w, conv_b)
    u, g = jnp.split(z, 2, axis=-1)
    return (jax.nn.gelu(g) * u) @ w_out

def first_inputs(seed: int = 0) -> dict:
    key = jax.random.key(seed)
    ks = jax.random.split(key, 24)
    f32 = jnp.float32
    nrm = lambda k, shape, s: jax.random.normal(k, shape, f32) * s
    u = jax.random.uniform(ks[16], (N_ODD, RNN_WIDTH), f32, minval=0.9, maxval=0.999)
    a0 = u ** (1.0 / RG_C)
    return {
        "x": nrm(ks[0], (BATCH, SEQ, D_MODEL), 1.0),
        "norm_mix": 1.0 + nrm(ks[1], (DEPTH, D_MODEL), 0.05),
        "norm_ffn": 1.0 + nrm(ks[2], (DEPTH, D_MODEL), 0.05),
        "pa_w_in": nrm(ks[3], (N_EVEN, D_MODEL, POOL_WIDTH + 3 * ATTN_WIDTH), D_MODEL ** -0.5),
        "pa_pool_w": nrm(ks[4], (N_EVEN, len(POOL_WINDOWS), POOL_GROUP, POOL_GROUP), POOL_GROUP ** -0.5),
        "pa_pool_scale": 1.0 + nrm(ks[5], (N_EVEN, POOL_WIDTH), 0.1),
        "pa_q_gain": 1.0 + nrm(ks[6], (N_EVEN, HEAD_DIM), 0.05),
        "pa_k_gain": 1.0 + nrm(ks[7], (N_EVEN, HEAD_DIM), 0.05),
        "pa_w_out": nrm(ks[8], (N_EVEN, POOL_WIDTH + ATTN_WIDTH, D_MODEL), (POOL_WIDTH + ATTN_WIDTH) ** -0.5),
        "rg_w_in": nrm(ks[9], (N_ODD, D_MODEL, 2 * RNN_WIDTH), D_MODEL ** -0.5),
        "rg_conv_w": nrm(ks[10], (N_ODD, RNN_CONV, RNN_WIDTH), RNN_CONV ** -0.5),
        "rg_conv_b": nrm(ks[11], (N_ODD, RNN_WIDTH), 0.01),
        "rg_w_a": nrm(ks[12], (N_ODD, RNN_BLOCKS, RNN_BLOCK, RNN_BLOCK), RNN_BLOCK ** -0.5),
        "rg_b_a": nrm(ks[13], (N_ODD, RNN_WIDTH), 0.01),
        "rg_w_x": nrm(ks[14], (N_ODD, RNN_BLOCKS, RNN_BLOCK, RNN_BLOCK), RNN_BLOCK ** -0.5),
        "rg_b_x": nrm(ks[15], (N_ODD, RNN_WIDTH), 0.01),
        "rg_lambda": jnp.log(a0) - jnp.log1p(-a0),
        "rg_w_out": nrm(ks[17], (N_ODD, RNN_WIDTH, D_MODEL), RNN_WIDTH ** -0.5),
        "ffn_w_in": nrm(ks[18], (DEPTH, D_MODEL, 2 * D_FF), D_MODEL ** -0.5),
        "ffn_conv_w": nrm(ks[19], (DEPTH, FFN_CONV, 2 * D_FF), FFN_CONV ** -0.5),
        "ffn_conv_b": nrm(ks[20], (DEPTH, 2 * D_FF), 0.01),
        "ffn_w_out": nrm(ks[21], (DEPTH, D_FF, D_MODEL), D_FF ** -0.5),
    }

def first_block(x, norm_mix, norm_ffn, pa_w_in, pa_pool_w, pa_pool_scale, pa_q_gain, pa_k_gain,
              pa_w_out, rg_w_in, rg_conv_w, rg_conv_b, rg_w_a, rg_b_a, rg_w_x, rg_b_x, rg_lambda,
              rg_w_out, ffn_w_in, ffn_conv_w, ffn_conv_b, ffn_w_out):
    for l in range(DEPTH):
        j = l // 2
        h = rms_norm(x, norm_mix[l])
        if l % 2 == 0:
            x = x + pool_attn_mixer(h, pa_w_in[j], pa_pool_w[j], pa_pool_scale[j],
                                    pa_q_gain[j], pa_k_gain[j], pa_w_out[j])
        else:
            x = x + rglru_mixer(h, rg_w_in[j], rg_conv_w[j], rg_conv_b[j], rg_w_a[j], rg_b_a[j],
                                rg_w_x[j], rg_b_x[j], rg_lambda[j], rg_w_out[j])
        h = rms_norm(x, norm_ffn[l])
        x = x + conv_ffn(h, ffn_w_in[l], ffn_conv_w[l], ffn_conv_b[l], ffn_w_out[l])
    return x


DEPTH_2 = 1

N_BRANCH = 4
D_MIX = D_MODEL // N_BRANCH
HEAD_A = 64
H_A = D_MIX // HEAD_A
LORA_W = 32
LORA_A = 32
LORA_V = 32
LORA_G = 64
LNX_EPS = 64e-5
CHUNK = 128
GROUP_B = 64
G_B = D_MIX // GROUP_B
CONV_K = 3
GROUP_D = 16
G_D = D_MIX // GROUP_D
N_STATE = 64
D_FF_2 = 4 * D_MODEL
LN_EPS = 1e-5

A_COLS = 3 * D_MIX + LORA_W + LORA_A + LORA_G
B_COLS = 2 * D_MIX
C_COLS = 3 * D_MIX
D_COLS = D_MIX
GATE_COLS = N_BRANCH * D_MODEL
OFF_B = A_COLS
OFF_C = OFF_B + B_COLS
OFF_D = OFF_C + C_COLS
OFF_G = OFF_D + D_COLS
N_IN = OFF_G + GATE_COLS


def rms_norm_2(x, g):
    xf = x.astype(jnp.float32)
    return xf * lax.rsqrt(jnp.mean(xf * xf, axis=-1, keepdims=True) + EPS) * g.astype(jnp.float32)

def layer_norm(x, w, b, eps):
    xf = x.astype(jnp.float32)
    mu = jnp.mean(xf, axis=-1, keepdims=True)
    var = jnp.mean(jnp.square(xf - mu), axis=-1, keepdims=True)
    return (xf - mu) * lax.rsqrt(var + eps) * w.astype(jnp.float32) + b.astype(jnp.float32)

def shift_prev(p):
    return jnp.pad(p, ((0, 0), (1, 0), (0, 0)))[:, :-1]

def wkv7(r, w, k, v, a, b):
    bsz, _, nh, n = r.shape

    def step(state, inp):
        r_t, w_t, k_t, v_t, a_t, b_t = inp
        sa = jnp.einsum('bhij,bhj->bhi', state, a_t)
        state = (state * w_t[:, :, None, :] + sa[..., None] * b_t[:, :, None, :]
                 + v_t[..., None] * k_t[:, :, None, :])
        return state, jnp.einsum('bhij,bhj->bhi', state, r_t)

    xs = tuple(jnp.moveaxis(t, 1, 0) for t in (r, w, k, v, a, b))
    s0 = jnp.zeros((bsz, nh, n, n), jnp.float32)
    _, out = lax.scan(step, s0, xs)
    return jnp.moveaxis(out, 0, 1)

def rwkv7_mixer(p, v_first, v_mix, mu, w0, w2, a0, a2, g2, k_k, k_a, r_k, lnx_w, lnx_b, w_out):
    bsz, seq, _ = p.shape
    p = p + (shift_prev(p) - p) * mu
    r = p[..., :D_MIX]
    k = p[..., D_MIX:2 * D_MIX]
    v = p[..., 2 * D_MIX:3 * D_MIX]
    wd = p[..., 3 * D_MIX:3 * D_MIX + LORA_W]
    ad = p[..., 3 * D_MIX + LORA_W:3 * D_MIX + LORA_W + LORA_A]
    gd = p[..., 3 * D_MIX + LORA_W + LORA_A:]
    log_w = -jax.nn.softplus(-(w0 + jnp.tanh(wd) @ w2)) - 0.5
    decay = jnp.exp(-jnp.exp(log_w))
    if v_mix is None:
        v_first = v
    else:
        v0, v1, v2 = v_mix
        v = v + (v_first - v) * jax.nn.sigmoid(v0 + (v @ v1) @ v2)
    a = jax.nn.sigmoid(a0 + ad @ a2)
    g = jax.nn.sigmoid(gd) @ g2

    def heads(t):
        return t.reshape(bsz, seq, H_A, HEAD_A).astype(jnp.float32)

    kk = heads(k * k_k)
    kk = kk / jnp.maximum(jnp.sqrt(jnp.sum(kk * kk, axis=-1, keepdims=True)), 1e-12)
    k = k * (1.0 + (a - 1.0) * k_a)
    rh, kh, vh, ah = heads(r), heads(k), heads(v), heads(a)
    o = wkv7(rh, heads(decay), kh, vh, -kk, kk * ah)
    o = layer_norm(o, lnx_w.reshape(H_A, HEAD_A), lnx_b.reshape(H_A, HEAD_A), LNX_EPS)
    o = o + jnp.sum(rh * kh * r_k, axis=-1, keepdims=True) * vh
    return (o.reshape(bsz, seq, D_MIX) * g) @ w_out, v_first

def spatial_gating_mixer(p, ln_w, ln_b, w_s, b_s, w_out):
    bsz, seq, _ = p.shape
    z = jax.nn.gelu(p)
    u = z[..., :D_MIX]
    v = layer_norm(z[..., D_MIX:], ln_w, ln_b, LN_EPS)
    v = v.reshape(bsz, seq // CHUNK, CHUNK, G_B, GROUP_B)
    mask = jnp.tril(jnp.ones((CHUNK, CHUNK), jnp.float32))
    mixed = jnp.einsum('gts,bnsgc->bntgc', w_s * mask, v) + b_s.T[None, None, :, :, None]
    return (u * mixed.reshape(bsz, seq, D_MIX)) @ w_out

def short_conv_mixer(p, conv_w, w_out):
    seq = p.shape[1]
    bg = p[..., :D_MIX]
    cg = p[..., D_MIX:2 * D_MIX]
    xin = p[..., 2 * D_MIX:]
    zp = jnp.pad(cg * xin, ((0, 0), (CONV_K - 1, 0), (0, 0)))
    y = sum(conv_w[j] * zp[:, j:j + seq] for j in range(CONV_K))
    return (bg * y) @ w_out

def _complex_affine_combine(e1, e2):
    a1r, a1i, b1r, b1i = e1
    a2r, a2i, b2r, b2i = e2
    return (a2r * a1r - a2i * a1i,
            a2r * a1i + a2i * a1r,
            a2r * b1r - a2i * b1i + b2r,
            a2r * b1i + a2i * b1r + b2i)

def s5_mixer(u, a_re, a_im, b_re, b_im, c_re, c_im, d, log_dt, glu_w):
    f32 = jnp.float32
    bsz, seq, _ = u.shape
    u32 = u.astype(f32)
    ug = u32.reshape(bsz, seq, G_D, GROUP_D)
    lam_re = jnp.minimum(a_re.astype(f32), -1e-4)
    lam_im = a_im.astype(f32)
    dt = jnp.exp(log_dt.astype(f32))[:, None]
    mag = jnp.exp(lam_re * dt)
    ab_re = mag * jnp.cos(lam_im * dt)
    ab_im = mag * jnp.sin(lam_im * dt)
    den = lam_re * lam_re + lam_im * lam_im
    q_re = ((ab_re - 1.0) * lam_re + ab_im * lam_im) / den
    q_im = (ab_im * lam_re - (ab_re - 1.0) * lam_im) / den
    bb_re = q_re[..., None] * b_re - q_im[..., None] * b_im
    bb_im = q_re[..., None] * b_im + q_im[..., None] * b_re
    bu_re = jnp.einsum('gnc,bsgc->bsgn', bb_re, ug)
    bu_im = jnp.einsum('gnc,bsgc->bsgn', bb_im, ug)
    ar = jnp.broadcast_to(ab_re, bu_re.shape)
    ai = jnp.broadcast_to(ab_im, bu_im.shape)
    _, _, x_re, x_im = lax.associative_scan(_complex_affine_combine, (ar, ai, bu_re, bu_im), axis=1)
    y = (jnp.einsum('gcn,bsgn->bsgc', c_re, x_re) - jnp.einsum('gcn,bsgn->bsgc', c_im, x_im))
    y = y.reshape(bsz, seq, D_MIX) + d * u32
    h = jax.nn.gelu(y) @ glu_w
    return h[..., :D_MODEL] * jax.nn.sigmoid(h[..., D_MODEL:])

def second_inputs(seed: int = 0) -> dict:
    key = jax.random.key(seed)
    ks = iter(jax.random.split(key, 64))
    f32 = jnp.float32
    L = DEPTH_2

    def nrm(shape, scale):
        return scale * jax.random.normal(next(ks), shape, f32)

    def uni(shape, lo, hi):
        return jax.random.uniform(next(ks), shape, f32, lo, hi)

    return {
        'x': nrm((BATCH, SEQ, D_MODEL), 1.0),
        'c': nrm((BATCH, D_MODEL), 1.0),
        'ada_w': nrm((L, D_MODEL, 6 * D_MODEL), 0.5 * D_MODEL ** -0.5),
        'ada_b': nrm((L, 6 * D_MODEL), 0.02),
        'norm_mix_g': 1.0 + nrm((L, D_MODEL), 0.1),
        'w_in': nrm((L, D_MODEL, N_IN), D_MODEL ** -0.5),
        'rwkv_mu': uni((L, A_COLS), 0.0, 1.0),
        'rwkv_w0': uni((L, D_MIX), -6.0, -1.0),
        'rwkv_w2': nrm((L, LORA_W, D_MIX), 0.1),
        'rwkv_a0': nrm((L, D_MIX), 0.1),
        'rwkv_a2': nrm((L, LORA_A, D_MIX), 0.1),
        'rwkv_g2': nrm((L, LORA_G, D_MIX), LORA_G ** -0.5),
        'rwkv_v0': 1.0 + nrm((L - 1, D_MIX), 0.1),
        'rwkv_v1': nrm((L - 1, D_MIX, LORA_V), D_MIX ** -0.5),
        'rwkv_v2': nrm((L - 1, LORA_V, D_MIX), 0.1),
        'rwkv_kk': 0.85 + nrm((L, D_MIX), 0.1),
        'rwkv_ka': 1.0 + nrm((L, D_MIX), 0.1),
        'rwkv_rk': nrm((L, H_A, HEAD_A), 0.1),
        'rwkv_lnx_w': 1.0 + nrm((L, D_MIX), 0.1),
        'rwkv_lnx_b': nrm((L, D_MIX), 0.02),
        'rwkv_out': nrm((L, D_MIX, D_MODEL), D_MIX ** -0.5),
        'sg_ln_w': 1.0 + nrm((L, D_MIX), 0.1),
        'sg_ln_b': nrm((L, D_MIX), 0.02),
        'sg_ws': nrm((L, G_B, CHUNK, CHUNK), CHUNK ** -0.5),
        'sg_bs': 1.0 + nrm((L, G_B, CHUNK), 0.1),
        'sg_out': nrm((L, D_MIX, D_MODEL), D_MIX ** -0.5),
        'conv_w': nrm((L, CONV_K, D_MIX), CONV_K ** -0.5),
        'conv_out': nrm((L, D_MIX, D_MODEL), D_MIX ** -0.5),
        's5_a_re': -0.5 + nrm((L, G_D, N_STATE), 0.01),
        's5_a_im': jnp.pi * jnp.arange(N_STATE, dtype=f32)[None, None, :] + nrm((L, G_D, N_STATE), 0.01),
        's5_b_re': nrm((L, G_D, N_STATE, GROUP_D), (2 * GROUP_D) ** -0.5),
        's5_b_im': nrm((L, G_D, N_STATE, GROUP_D), (2 * GROUP_D) ** -0.5),
        's5_c_re': nrm((L, G_D, GROUP_D, N_STATE), (2 * N_STATE) ** -0.5),
        's5_c_im': nrm((L, G_D, GROUP_D, N_STATE), (2 * N_STATE) ** -0.5),
        's5_d': nrm((L, D_MIX), 1.0),
        's5_log_dt': uni((L, G_D), math.log(1e-3), math.log(1e-1)),
        's5_glu_w': nrm((L, D_MIX, 2 * D_MODEL), D_MIX ** -0.5),
        'w_o': nrm((L, D_MODEL, D_MODEL), D_MODEL ** -0.5),
        'norm_ffn_g': 1.0 + nrm((L, D_MODEL), 0.1),
        'ffn_w1': nrm((L, D_MODEL, D_FF_2), D_MODEL ** -0.5),
        'ffn_w2': nrm((L, D_FF_2, D_MODEL), D_FF_2 ** -0.5),
        'final_g': 1.0 + nrm((D_MODEL,), 0.1),
    }

def second_block(x, c, ada_w, ada_b, norm_mix_g, w_in, rwkv_mu, rwkv_w0, rwkv_w2, rwkv_a0, rwkv_a2,
              rwkv_g2, rwkv_v0, rwkv_v1, rwkv_v2, rwkv_kk, rwkv_ka, rwkv_rk, rwkv_lnx_w, rwkv_lnx_b,
              rwkv_out, sg_ln_w, sg_ln_b, sg_ws, sg_bs, sg_out, conv_w, conv_out, s5_a_re, s5_a_im,
              s5_b_re, s5_b_im, s5_c_re, s5_c_im, s5_d, s5_log_dt, s5_glu_w, w_o, norm_ffn_g,
              ffn_w1, ffn_w2, final_g):
    in_dtype = x.dtype
    bsz, seq, _ = x.shape
    c_act = jax.nn.silu(c.astype(jnp.float32))
    v_first = None
    for l in range(DEPTH_2):
        mod = (c_act @ ada_w[l] + ada_b[l])[:, None, :]
        sh1, sc1, gt1, sh2, sc2, gt2 = jnp.split(mod, 6, axis=-1)

        h = rms_norm_2(x, norm_mix_g[l]) * (1.0 + sc1) + sh1
        p = h @ w_in[l]
        v_mix = None if l == 0 else (rwkv_v0[l - 1], rwkv_v1[l - 1], rwkv_v2[l - 1])
        y_a, v_first = rwkv7_mixer(p[..., :OFF_B], v_first, v_mix, rwkv_mu[l], rwkv_w0[l], rwkv_w2[l],
                                   rwkv_a0[l], rwkv_a2[l], rwkv_g2[l], rwkv_kk[l], rwkv_ka[l],
                                   rwkv_rk[l], rwkv_lnx_w[l], rwkv_lnx_b[l], rwkv_out[l])
        y_b = spatial_gating_mixer(p[..., OFF_B:OFF_C], sg_ln_w[l], sg_ln_b[l], sg_ws[l], sg_bs[l], sg_out[l])
        y_c = short_conv_mixer(p[..., OFF_C:OFF_D], conv_w[l], conv_out[l])
        y_d = s5_mixer(p[..., OFF_D:OFF_G], s5_a_re[l], s5_a_im[l], s5_b_re[l], s5_b_im[l],
                       s5_c_re[l], s5_c_im[l], s5_d[l], s5_log_dt[l], s5_glu_w[l])
        gates = jax.nn.sigmoid(p[..., OFF_G:]).reshape(bsz, seq, N_BRANCH, D_MODEL)
        merged = (gates[:, :, 0] * y_a + gates[:, :, 1] * y_b
                  + gates[:, :, 2] * y_c + gates[:, :, 3] * y_d)
        x = x + gt1 * (merged @ w_o[l])

        h = rms_norm_2(x, norm_ffn_g[l]) * (1.0 + sc2) + sh2
        x = x + gt2 * (jnp.square(jax.nn.relu(h @ ffn_w1[l])) @ ffn_w2[l])
    return rms_norm_2(x, final_g).astype(in_dtype)


def setup_inputs(seed=0):
    out = dict(first_inputs(seed))
    for name, value in second_inputs(seed + 1).items():
        if name != "x":
            out[name + "_2"] = value
    return out


def reference(
    x, norm_mix, norm_ffn, pa_w_in, pa_pool_w, pa_pool_scale, pa_q_gain, pa_k_gain, pa_w_out,
    rg_w_in, rg_conv_w, rg_conv_b, rg_w_a, rg_b_a, rg_w_x, rg_b_x, rg_lambda, rg_w_out,
    ffn_w_in, ffn_conv_w, ffn_conv_b, ffn_w_out, c_2, ada_w_2, ada_b_2, norm_mix_g_2, w_in_2,
    rwkv_mu_2, rwkv_w0_2, rwkv_w2_2, rwkv_a0_2, rwkv_a2_2, rwkv_g2_2, rwkv_v0_2, rwkv_v1_2,
    rwkv_v2_2, rwkv_kk_2, rwkv_ka_2, rwkv_rk_2, rwkv_lnx_w_2, rwkv_lnx_b_2, rwkv_out_2,
    sg_ln_w_2, sg_ln_b_2, sg_ws_2, sg_bs_2, sg_out_2, conv_w_2, conv_out_2, s5_a_re_2,
    s5_a_im_2, s5_b_re_2, s5_b_im_2, s5_c_re_2, s5_c_im_2, s5_d_2, s5_log_dt_2, s5_glu_w_2,
    w_o_2, norm_ffn_g_2, ffn_w1_2, ffn_w2_2, final_g_2,
):
    x = first_block(
        x, norm_mix, norm_ffn, pa_w_in, pa_pool_w, pa_pool_scale, pa_q_gain, pa_k_gain,
        pa_w_out, rg_w_in, rg_conv_w, rg_conv_b, rg_w_a, rg_b_a, rg_w_x, rg_b_x, rg_lambda,
        rg_w_out, ffn_w_in, ffn_conv_w, ffn_conv_b, ffn_w_out,
    )
    return second_block(
        x, c_2, ada_w_2, ada_b_2, norm_mix_g_2, w_in_2, rwkv_mu_2, rwkv_w0_2, rwkv_w2_2,
        rwkv_a0_2, rwkv_a2_2, rwkv_g2_2, rwkv_v0_2, rwkv_v1_2, rwkv_v2_2, rwkv_kk_2, rwkv_ka_2,
        rwkv_rk_2, rwkv_lnx_w_2, rwkv_lnx_b_2, rwkv_out_2, sg_ln_w_2, sg_ln_b_2, sg_ws_2,
        sg_bs_2, sg_out_2, conv_w_2, conv_out_2, s5_a_re_2, s5_a_im_2, s5_b_re_2, s5_b_im_2,
        s5_c_re_2, s5_c_im_2, s5_d_2, s5_log_dt_2, s5_glu_w_2, w_o_2, norm_ffn_g_2, ffn_w1_2,
        ffn_w2_2, final_g_2,
    )


_drawn_inputs = setup_inputs


def setup_inputs(seed=0):
    import zlib

    import numpy as np

    out = dict(_drawn_inputs(seed))
    spreads = {}
    factors = {'pa_q_gain': 5.107,
     'pa_k_gain': 5.546,
     'rg_conv_b': 2.992,
     'rg_b_a': 64.0,
     'rg_b_x': 47.717,
     'ffn_conv_b': 5.204,
     'rwkv_w2_2': 8.0,
     'rwkv_a0_2': 8.0,
     'rwkv_a2_2': 4.32,
     'rwkv_kk_2': 26.56,
     'rwkv_ka_2': 6.289,
     'rwkv_rk_2': 3.112,
     'rwkv_lnx_w_2': 8.0,
     'rwkv_lnx_b_2': 64.0,
     'sg_ln_w_2': 8.0,
     'sg_ln_b_2': 64.0,
     'sg_bs_2': 7.443,
     's5_a_re_2': 64.0,
     's5_a_im_2': 64.0,
     's5_b_re_2': 64.0,
     's5_b_im_2': 64.0,
     's5_c_re_2': 64.0,
     's5_c_im_2': 64.0,
     's5_log_dt_2': 64.0}
    for name, (base, spread) in spreads.items():
        noise = np.random.default_rng([zlib.crc32(name.encode()), seed]).standard_normal(out[name].shape)
        drawn = base * np.exp(spread * noise) if base else spread * noise
        out[name] = __import__('jax').numpy.asarray(drawn.astype(out[name].dtype))
    for name, factor in factors.items():
        out[name] = (out[name] * factor).astype(out[name].dtype)
    return out
```

```python
from contextlib import ExitStack

import concourse.bass as bass
import numpy as np
from concourse import mybir

F32 = mybir.dt.float32
ALU = mybir.AluOpType
ACT = mybir.ActivationFunctionType
AX = mybir.AxisListType.X
NEG = mybir.AluOpType.subtract
T = 256
TWO_PI = 6.283185307179586
ROUND = 12582912.0

VECS = [
    ("norm_mix0", 8), ("norm_mix1", 8), ("norm_ffn0", 8), ("norm_ffn1", 8), ("pool_scale", 4),
    ("q_gain", 1), ("k_gain", 1), ("rg_cw", 40), ("rg_cb", 10), ("rg_ba", 10), ("rg_bx", 10),
    ("rg_lam", 10), ("ffn_cw0", 132), ("ffn_cw1", 132), ("ffn_cb0", 44), ("ffn_cb1", 44),
    ("c", 8), ("ada_b", 48), ("norm_mix2", 8), ("mu", 7), ("w0", 2), ("a0", 2), ("kk", 2), ("ka", 2),
    ("rk", 2), ("lnw", 2), ("lnb", 2), ("sglw", 2), ("sglb", 2), ("cw", 6), ("s_are", 8), ("s_aim", 8),
    ("s_ldt", 8), ("s_d", 2), ("norm_ffn2", 8), ("final_g", 8),
]
VOFF, NVEC = {}, 0
for _n, _c in VECS:
    VOFF[_n] = NVEC
    NVEC += _c

CONSTS = [
    ("ident", 128), ("ones", 128), ("blk", 128), ("dm", 384), ("invc", 1024), ("su", 128), ("iu", 128),
    ("l0", 128), ("l0t", 128), ("l1", 128), ("l2", 128), ("l3", 128), ("l4", 128), ("l5", 128),
    ("smask", 256), ("iota", 256), ("sgm", 128), ("bmask", 8), ("cmask", 32),
]
COFF, NCONST = {}, 0
for _n, _c in CONSTS:
    COFF[_n] = NCONST
    NCONST += _c


def const_array():
    c = {}
    i = np.arange(128)
    s, t = i[:, None], i[None, :]
    c["ident"] = np.eye(128)
    c["ones"] = np.ones((128, 128))
    c["blk"] = s // 64 == t // 64
    q, k = i[:, None], np.arange(256)[None, :]
    lo = np.where(k[:, :128] <= q, k[:, :128] - q, -1e34)
    hi = np.where(k <= q + 128, k - (q + 128), -1e34)
    c["dm"] = np.concatenate([lo, hi], 1)
    n = np.arange(1, 257)
    c["invc"] = np.tile(np.concatenate([1.0 / np.minimum(n, w) for w in (2, 4, 8, 16)]), (128, 1))
    same = s // 64 == t // 64
    c["su"] = same & (s < t)
    c["iu"] = same & (s <= t)
    for v in range(6):
        m = (s >> (v + 1) == t >> (v + 1)) & ((s >> v) % 2 == 0) & ((t >> v) % 2 == 1)
        c[f"l{v}"] = m
        if v == 0:
            c["l0t"] = m.T
    c["smask"] = np.tile(np.arange(256) % 64 != 0, (128, 1))
    c["iota"] = np.tile(np.arange(256), (128, 1))
    c["sgm"] = s <= t
    g = i // 16
    c["bmask"] = g[:, None] == np.arange(8)[None, :]
    st = np.zeros((128, 4, 8))
    for j in range(4):
        st[:, j] = (2 * j + i // 64)[:, None] == np.arange(8)[None, :]
    c["cmask"] = st.reshape(128, 32)
    return np.ascontiguousarray(np.concatenate([np.asarray(c[n], np.float32) for n, _ in CONSTS], 1))


class Queue:

    def __init__(self, sem):
        self.sem, self.n, self.ops, self.seen = sem, 0, [], {}

    def wait(self, *toks):
        for tok in toks:
            if tok is None:
                continue
            if isinstance(tok, list):
                self.wait(*tok)
                continue
            sem, v = tok
            if self.seen.get(id(sem), 0) < v:
                self.seen[id(sem)] = v
                self.ops.append(lambda e, sem=sem, v=v: e.wait_ge(sem, v))

    def quiet(self, f, *toks):
        self.wait(*toks)
        self.ops.append(f)

    def run(self, f, *toks):
        self.wait(*toks)
        self.n += 1
        self.ops.append(lambda e: f(e).then_inc(self.sem, 1))
        return (self.sem, self.n)

    def dma(self, out, in_, sem, *toks):
        self.wait(*toks)
        self.ops.append(lambda e: e.dma_start(out, in_).then_inc(sem, 16))

    def play(self, e):
        for op in self.ops:
            op(e)


def split8(nk):
    n = -(-nk // 8)
    return [nk // n + (i < nk % n) for i in range(n)]


def build(nc, d, out, dbg=None):
    with ExitStack() as ctx:
        cnt = [0]

        def alloc(stack, name, shape, dt=F32):
            cnt[0] += 1
            return stack.enter_context(nc.sbuf_tensor(f"{name}_{cnt[0]}", shape, dt))

        def sem(name):
            return ctx.enter_context(nc.semaphore(name))

        PE, V, A, G, SP = (Queue(sem(n)) for n in ("s_pe", "s_dve", "s_act", "s_pool", "s_sp"))
        ps = [ctx.enter_context(nc.psum_tensor(f"ps{i}", [128, 512], F32)) for i in range(8)]

        free = [None] * 8
        held = [False] * 8
        turn = [0]

        def bank():
            b = turn[0] % 8
            while held[b]:
                turn[0] += 1
                b = turn[0] % 8
            turn[0] += 1
            held[b] = True
            PE.wait(free[b])
            return b, ps[b]

        def done(b, tok):
            held[b] = False
            free[b] = tok

        cst = alloc(ctx, "cst", [128, NCONST])
        vec = alloc(ctx, "vec", [128, NVEC])
        s_c = sem("s_c")
        s_par = sem("s_par")
        x = alloc(ctx, "x", [128, 8, T])
        h = alloc(ctx, "h", [128, 8, T])
        s_x = sem("s_x")
        A.dma(x[:, :, :], d["xT"], s_x)
        A.dma(cst[:, :], d["cst"], s_c)
        A.dma(vec[:, :], d["vec"], s_c)
        t_x, t_c = (s_x, 16), (s_c, 32)

        def C(name, lo=0, hi=None):
            n = dict(CONSTS)[name]
            return cst[:, COFF[name] + lo:COFF[name] + (n if hi is None else hi)]

        def P(name, i=0, n=1):
            return vec[:, VOFF[name] + i:VOFF[name] + i + n]

        NS = 9
        ring = [alloc(ctx, f"ring{i}", [128, 8, 128]) for i in range(NS)]
        rsem = [sem(f"s_ring{i}") for i in range(NS)]
        rfree = [None] * NS
        rn = [0]

        def load(src, nk):
            i = rn[0] % NS
            use = rn[0] // NS + 1
            rn[0] += 1
            SP.dma(ring[i][:, 0:nk, :], src, rsem[i], rfree[i])
            return i, (rsem[i], 16 * use)

        def linear(w, m, rhs, nk, o, toks, start=True, stop=True):
            k = 0
            for n in split8(nk):
                i, tok = load(w[m, :, k:k + n, :], n)
                PE.wait(tok, *toks)
                for q in range(n):
                    f = (lambda e, i=i, q=q, k=k: e.matmul(
                        o, ring[i][:, q, :], rhs(k + q), start=start and k + q == 0,
                        stop=stop and k + q == nk - 1))
                    if q == n - 1:
                        rfree[i] = PE.run(lambda e, f=f: f(e))
                    else:
                        PE.quiet(f)
                k += n
            return rfree[i]

        def mm(o, l, r, *toks, start=True, stop=True, last=True):
            f = lambda e: e.matmul(o, l, r, start=start, stop=stop)
            return PE.run(f, *toks) if last else PE.quiet(f, *toks)

        def act(o, i, func, *toks, scale=1.0, bias=0.0, acc=None):
            return A.run(lambda e: e.activation(o, i, func, bias=bias, scale=scale, accum_out=acc), *toks)

        def tt(o, a, b, op, *toks, q=None):
            return (q or V).run(lambda e: e.tensor_tensor(o, a, b, op), *toks)

        def ts(o, a, s1, s2, op0, op1, *toks, q=None):
            if s2 is None:
                return (q or V).run(lambda e: e.tensor_scalar(o, a, s1, None, op0), *toks)
            return (q or V).run(lambda e: e.tensor_scalar(o, a, s1, s2, op0, op1), *toks)

        def stt(o, a, s, b, op0, op1, *toks):
            return V.run(lambda e: e.scalar_tensor_tensor(out=o, in0=a, scalar=s, in1=b, op0=op0, op1=op1), *toks)

        def copy(o, i, *toks, q=None):
            q = q or V
            if q is A:
                return act(o, i, ACT.Copy, *toks)
            return q.run(lambda e: e.tensor_copy(o, i), *toks)

        def recip(o, i, *toks):
            return V.run(lambda e: e.reciprocal(o, i), *toks)

        MUL, ADD, SUB, MAX, MIN = ALU.mult, ALU.add, ALU.subtract, ALU.max, ALU.min
        ones, blk, ident = C("ones"), C("blk"), C("ident")
        for q in (PE, V, A, G):
            q.wait(t_c)

        rst = alloc(ctx, "rst", [128, T])
        h_free = [None]

        def norm_stats(t_in):
            t_sq = act(h[:, :, :], x[:, :, :], ACT.Square, t_in, h_free[0])
            b, p = bank()
            for k in range(8):
                t = mm(p[:, 0:T], ones, h[:, k, :], t_sq, start=k == 0, stop=k == 7, last=k == 7)
            t = ts(rst[:, :], p[:, 0:T], 1.0 / 1024, 1e-6, MUL, ADD, t)
            done(b, t)
            t = act(rst[:, :], rst[:, :], ACT.Sqrt, t)
            return recip(rst[:, :], rst[:, :], t)

        def norm(gain, t_in):
            t = norm_stats(t_in)
            toks = [stt(h[:, k, :], x[:, k, :], P(gain, k), rst[:, :], MUL, MUL, t) for k in range(8)]
            return toks[-1]

        def residual(w, nk, rhs, toks, scale=None):
            for m in range(8):
                b, p = bank()
                t = linear(w, m, rhs, nk, p[:, 0:T], toks)
                if scale is None:
                    t = tt(x[:, m, :], p[:, 0:T], x[:, m, :], ADD, t)
                else:
                    t = stt(x[:, m, :], p[:, 0:T], scale(m), x[:, m, :], MUL, ADD, t)
                done(b, t)
            return t

        def hk(k):
            return h[:, k, :]

        dbgs = []

        def dump(name, ap, tok):
            if dbg is not None and name in dbg:
                s = sem("dbg_" + name)
                A.dma(dbg[name], ap, s, tok)
                dbgs.append((s, 16))
                for q in (V, PE, A, G):
                    q.wait((s, 16))

        def pool_attn(t_x):
            t_h = norm("norm_mix0", t_x)
            with ExitStack() as st:
                u = alloc(st, "u", [128, 4, 16 + T])
                qk = alloc(st, "qk", [128, 8, T])
                sq = alloc(st, "sq", [128, 8, T])
                rq = alloc(st, "rq", [128, 2, T])
                vt = alloc(st, "vt", [128, 2, 512])
                pa = alloc(st, "pa", [128, 8, T])
                ta = alloc(st, "ta", [128, 16 + T])
                tb = alloc(st, "tb", [128, 16 + T])
                pw = alloc(st, "pw", [128, 4, 128])
                gq = alloc(st, "gq", [128, 1])
                A.dma(pw[:, :, :], d["pool_w"], s_par)
                t_pw = (s_par, 16)
                t0 = V.run(lambda e: e.memset(u[:, :, 0:16], 0.0), t_h)
                t0 = V.run(lambda e: e.memset(ta[:, 0:16], 0.0))
                t0 = V.run(lambda e: e.memset(tb[:, 0:16], 0.0))
                t_g = ts(gq[:, :], P("q_gain"), 0.125, None, MUL, None)
                t_qk = []
                for m in range(4, 12):
                    i = m - 4
                    b, p = bank()
                    t = linear(d["pa_w_in"], m, hk, 8, p[:, 0:T], [t_h])
                    t1 = act(sq[:, i, :], p[:, 0:T], ACT.Square, t)
                    b2, p2 = bank()
                    t2 = mm(p2[:, 0:T], blk, sq[:, i, :], t1)
                    r = rq[:, i % 2, :]
                    t = ts(r, p2[:, 0:T], 1.0 / 64, 1e-6, MUL, ADD, t2, t_qk[i - 2] if i > 1 else None)
                    done(b2, t)
                    t = act(r, r, ACT.Sqrt, t)
                    t = recip(r, r, t)
                    t = stt(qk[:, i, :], p[:, 0:T], gq[:, :] if i < 4 else P("k_gain"), r, MUL, MUL, t, t_g)
                    done(b, t)
                    t_qk.append(t)
                t_u = []
                for m in range(4):
                    b, p = bank()
                    t = linear(d["pa_w_in"], m, hk, 8, p[:, 0:T], [t_h])
                    t = copy(u[:, m, 16:], p[:, 0:T], t, q=A)
                    done(b, t)
                    t_u.append(t)
                bs = [bank(), bank()]
                for m in range(12, 16):
                    i, tok = load(d["pa_w_in"][m, :, 0:8, :], 8)
                    PE.wait(tok)
                    for z in range(2):
                        o = bs[z][1][:, (m - 12) * 128:(m - 11) * 128]
                        for k in range(8):
                            t = mm(o, h[:, k, z * 128:(z + 1) * 128], ring[i][:, k, :], start=k == 0,
                                   stop=k == 7, last=k == 7)
                    rfree[i] = t
                t_v = []
                for z in range(2):
                    tv = copy(vt[:, z, :], bs[z][1][:, :], t, q=A)
                    done(bs[z][0], tv)
                    t_v.append(tv)
                h_free[0] = t
                prev = t0
                for g in range(4):
                    cur, t = u[:, g, :], t_u[g]
                    for w in range(g + 1):
                        s = 1 << w
                        nxt = (ta, tb)[w % 2]
                        t = tt(nxt[:, 16:], cur[:, 16:], cur[:, 16 - s:16 + T - s], ADD, t, prev)
                        cur = nxt
                        prev = None
                    t = tt(cur[:, 16:], cur[:, 16:], C("invc", g * T, (g + 1) * T), MUL, t)
                    t = tt(sq[:, g, :], cur[:, 16:], u[:, g, 16:], SUB, t, (PE.sem, PE.n))
                    prev = t
                    b, p = bank()
                    t = mm(p[:, 0:T], pw[:, g, :], sq[:, g, :], t, t_pw)
                    t = act(pa[:, g, :], p[:, 0:T], ACT.Copy, t, scale=P("pool_scale", g))
                    done(b, t)
                t_p = t
                L = alloc(st, "L", [128, 2, 384])
                PT = alloc(st, "PT", [128, 2, 384])
                sm = alloc(st, "sm", [128, 2, 8])
                t_pt = [None, None]
                for hd in range(8):
                    j, r, z = hd // 2, 64 * (hd % 2), hd % 2
                    b, p = bank()
                    qh, kh = qk[r:r + 64, j, :], qk[r:r + 64, 4 + j, :]
                    mm(p[:, 0:128], qh[:, 0:128], kh[:, 0:128], t_qk[-1], last=False)
                    t = mm(p[:, 128:384], qh[:, 128:256], kh)
                    slope = 2.0 ** (-8.0 * (hd + 1) / 8)
                    t = stt(L[:, z, :], C("dm"), slope, p[:, 0:384], MUL, ADD, t, t_pt[z])
                    done(b, t)
                    s = sm[:, z, :]
                    t1 = V.run(lambda e, z=z, s=s: e.tensor_reduce(s[:, 0:1], L[:, z, 0:128], AX, MAX, negate=True), t)
                    t2 = V.run(lambda e, z=z, s=s: e.tensor_reduce(s[:, 1:2], L[:, z, 128:384], AX, MAX, negate=True), t)
                    t1 = act(L[:, z, 0:128], L[:, z, 0:128], ACT.Exp, t1, bias=s[:, 0:1], acc=s[:, 2:3])
                    t2 = act(L[:, z, 128:384], L[:, z, 128:384], ACT.Exp, t2, bias=s[:, 1:2], acc=s[:, 3:4])
                    t = recip(s[:, 4:6], s[:, 2:4], t2)
                    ts(L[:, z, 0:128], L[:, z, 0:128], s[:, 4:5], None, MUL, None, t)
                    t = ts(L[:, z, 128:384], L[:, z, 128:384], s[:, 5:6], None, MUL, None)
                    b, p = bank()
                    for n in range(3):
                        t3 = PE.run(lambda e, p=p, z=z, n=n: e.transpose(
                            p[:, n * 128:(n + 1) * 128], L[:, z, n * 128:(n + 1) * 128], ident), t)
                    t_pt[z] = copy(PT[:, z, :], p[:, 0:384], t3, q=A)
                    done(b, t_pt[z])
                    b, p = bank()
                    o = p[r:r + 64, :]
                    mm(o[:, 0:256], vt[:, 0, hd * 64:hd * 64 + 64], PT[:, z, 0:256], t_pt[z], t_v, last=False, stop=False)
                    t = mm(o[:, 128:256], vt[:, 1, hd * 64:hd * 64 + 64], PT[:, z, 256:384], start=False)
                    t_pt[z] = copy(pa[r:r + 64, 4 + j, :], o[:, 0:256], t, q=A)
                    done(b, t_pt[z])
                dump("pa", pa[:, :, :], t_pt[1])
                return residual(d["pa_w_out"], 8, lambda k: pa[:, k, :], [t_p, t_pt[1]])

        def conv_taps(z, src, wname, nm, m, taps, t, bias):
            t = act(z, src, ACT.Identity, t, scale=P(wname, (taps - 1) * nm + m), bias=bias)
            for s in range(1, taps):
                t = stt(z[:, s:], src[:, 0:T - s], P(wname, (taps - 1 - s) * nm + m), z[:, s:], MUL, ADD, t)
            return t

        def conv_ffn(l, t_x):
            t_h = norm(f"norm_ffn{l}", t_x)
            with ExitStack() as st:
                hid = alloc(st, "hid", [128, 22, T])
                zu = alloc(st, "zu", [128, 2, T])
                zg = alloc(st, "zg", [128, 2, T])
                old = [None, None]
                V.wait(t_h)
                A.wait(t_h)
                for m in range(22):
                    b, p = bank()
                    t = linear(d[f"ffn_w_in{l}"], m, hk, 8, p[:, 0:T], [t_h])
                    tu = conv_taps(zu[:, m % 2, :], p[:, 0:T], f"ffn_cw{l}", 44, m, 3, [t, old[m % 2]],
                                   P(f"ffn_cb{l}", m))
                    done(b, tu)
                    b, p = bank()
                    t = linear(d[f"ffn_w_in{l}"], m + 22, hk, 8, p[:, 0:T], [t_h])
                    tg = conv_taps(zg[:, m % 2, :], p[:, 0:T], f"ffn_cw{l}", 44, m + 22, 3, t,
                                   P(f"ffn_cb{l}", m + 22))
                    done(b, tg)
                    t = act(zg[:, m % 2, :], zg[:, m % 2, :], ACT.Gelu_apprx_tanh, tg)
                    t = tt(hid[:, m, :], zg[:, m % 2, :], zu[:, m % 2, :], MUL, t)
                    old[m % 2] = t
                h_free[0] = (PE.sem, PE.n)
                return residual(d[f"ffn_w_out{l}"], 22, lambda k: hid[:, k, :], [t])

        def rglru(t_x):
            t_h = norm("norm_mix1", t_x)
            with ExitStack() as st:
                gate = alloc(st, "gate", [128, 10, T])
                xr = alloc(st, "xr", [128, 10, T])
                rr = alloc(st, "rr", [128, 10, T])
                ii = alloc(st, "ii", [128, 10, T])
                wab = alloc(st, "wab", [128, 20, 128])
                cf = alloc(st, "cf", [128, 8, 10])
                V.wait(t_h)
                A.wait(t_h)
                s_w = sem("s_wab")
                A.dma(wab[:, :, :], d["rg_wab"], s_w)
                t_w = (s_w, 16)
                lam = P("rg_lam", 0, 10)
                c = [cf[:, n, :] for n in range(8)]
                t = ts(c[0], lam, -1.0, 0.0, MUL, MAX)
                t = ts(c[1], lam, -1.0, None, MUL, None)
                t = tt(c[1], c[1], lam, MIN, t)
                t = act(c[1], c[1], ACT.Exp, t)
                t = ts(c[2], c[1], 2.0, None, ADD, None, t)
                t = recip(c[2], c[2], t)
                t = tt(c[1], c[1], c[2], MUL, t)
                t = tt(c[2], c[1], c[1], MUL, t)
                t = ts(c[3], c[2], 1.0 / 17, 1.0 / 15, MUL, ADD, t)
                for n in (13, 11, 9, 7, 5, 3, 1):
                    t = tt(c[3], c[3], c[2], MUL, t)
                    t = ts(c[3], c[3], 1.0 / n, None, ADD, None, t)
                t = tt(c[3], c[3], c[1], MUL, t)
                t = stt(c[3], c[3], 2.0, c[0], MUL, ADD, t)
                t_cf = ts(c[4], c[3], -8.0, None, MUL, None, t)
                t_cf = ts(c[5], c[3], 8.0, None, MUL, None, t)
                tx = []
                for m in range(10):
                    b, p = bank()
                    t = linear(d["rg_w_in"], m + 10, hk, 8, p[:, 0:T], [t_h])
                    t = conv_taps(xr[:, m, :], p[:, 0:T], "rg_cw", 10, m, 4, t, P("rg_cb", m))
                    done(b, t)
                    tx.append(t)
                tr = []
                for m in range(10):
                    b, p = bank()
                    t = mm(p[:, 0:T], wab[:, m, :], xr[:, m, :], tx[m], t_w)
                    t = act(rr[:, m, :], p[:, 0:T], ACT.Sigmoid, t, bias=P("rg_ba", m))
                    done(b, t)
                    b, p = bank()
                    t = mm(p[:, 0:T], wab[:, 10 + m, :], xr[:, m, :])
                    t = act(ii[:, m, :], p[:, 0:T], ACT.Sigmoid, t, bias=P("rg_bx", m))
                    done(b, t)
                    tr.append(tt(ii[:, m, :], ii[:, m, :], xr[:, m, :], MUL, t))
                tg = []
                for m in range(10):
                    b, p = bank()
                    t = linear(d["rg_w_in"], m, hk, 8, p[:, 0:T], [t_h])
                    t = copy(gate[:, m, :], p[:, 0:T], t)
                    done(b, t)
                    tg.append(t)
                h_free[0] = (PE.sem, PE.n)
                th = []
                for m in range(10):
                    t = act(xr[:, m, :], rr[:, m, :], ACT.Tanh, tr[m], t_cf, scale=c[5][:, m:m + 1])
                    t = act(rr[:, m, :], rr[:, m, :], ACT.Exp, t, scale=c[4][:, m:m + 1])
                    th.append(t)
                sc = alloc(st, "sc", [128, 2, T])
                t_sc = [None, None]
                tq = []
                for m in range(10):
                    s = sc[:, m % 2, :]
                    t = ts(s, xr[:, m, :], 1.0, None, ADD, None, th[m], t_sc[m % 2])
                    t = recip(s, s, t)
                    t = stt(xr[:, m, :], xr[:, m, :], 2.0, s, MUL, MUL, t)
                    t_sc[m % 2] = t
                    tq.append(act(xr[:, m, :], xr[:, m, :], ACT.Sqrt, t))
                ty = []
                for m in range(10):
                    t = act(gate[:, m, :], gate[:, m, :], ACT.Gelu_apprx_tanh, tg[m])
                    t2 = tt(ii[:, m, :], ii[:, m, :], xr[:, m, :], MUL, tq[m])
                    t2 = V.run(lambda e, m=m: e.tensor_tensor_scan(xr[:, m, :], rr[:, m, :], ii[:, m, :], 0.0, MUL, ADD), t2)
                    ty.append(tt(gate[:, m, :], gate[:, m, :], xr[:, m, :], MUL, t, t2))
                dump("y1", gate[:, :, :], ty[-1])
                return residual(d["rg_w_out"], 10, lambda k: gate[:, k, :], [ty[-1]])

        cosT = alloc(ctx, "cosT", [128, 8, T])
        sinT = alloc(ctx, "sinT", [128, 8, T])
        s5p = alloc(ctx, "s5p", [128, 20, 8])
        mod = alloc(ctx, "mod", [128, 48])
        gsc = alloc(ctx, "gsc", [128, 2, 8])

        def round_off(a, tmp, t):
            t = ts(tmp, a, ROUND, ROUND, ADD, SUB, t)
            return tt(a, a, tmp, SUB, t)

        def s5_params():
            with ExitStack() as st:
                w = alloc(st, "w", [128, 8, T])
                tmp = alloc(st, "tmp", [128, 8, T])
                c = [s5p[:, n, :] for n in range(20)]
                V.wait((PE.sem, PE.n), (A.sem, A.n))
                dt, lr, mag, ph, qre, qim = c[0], c[1], c[2], c[3], c[4], c[5]
                t = act(dt, P("s_ldt", 0, 8), ACT.Exp)
                t = ts(lr, P("s_are", 0, 8), -1e-4, None, MIN, None, t)
                t = tt(mag, lr, dt, MUL, t)
                t = act(mag, mag, ACT.Exp, t)
                t = tt(c[6], P("s_aim", 0, 8), dt, MUL, t)
                t = ts(c[7], c[6], 1.0 / TWO_PI, None, MUL, None, t)
                t = ts(c[7], c[7], ROUND, ROUND, ADD, SUB, t)
                c1 = 6.28125
                c2 = float(np.float32(0.0019340515136718750))
                c3 = TWO_PI - c1 - c2
                for v in (c1, c2, c3):
                    t = stt(c[6], c[7], -v, c[6], MUL, ADD, t)
                t = ts(ph, c[6], 1.0 / TWO_PI, None, MUL, None, t)
                t = round_off(ph, c[7], t)
                t = ts(c[8], ph, 0.25, None, ADD, None, t)
                t = round_off(c[8], c[7], t)
                t = act(c[8], c[8], ACT.Sin, t, scale=6.283185)
                t = act(c[9], ph, ACT.Sin, t, scale=6.283185)
                t = tt(c[8], c[8], mag, MUL, t)
                t = ts(c[8], c[8], 1.0, None, SUB, None, t)
                t = tt(c[9], c[9], mag, MUL, t)
                li = P("s_aim", 0, 8)
                t = tt(c[10], lr, lr, MUL, t)
                t = tt(c[11], li, li, MUL, t)
                t = tt(c[10], c[10], c[11], ADD, t)
                t = recip(c[10], c[10], t)
                t = tt(c[11], c[8], lr, MUL, t)
                t = tt(c[12], c[9], li, MUL, t)
                t = tt(c[11], c[11], c[12], ADD, t)
                t = tt(qre, c[11], c[10], MUL, t)
                t = tt(c[11], c[9], lr, MUL, t)
                t = tt(c[12], c[8], li, MUL, t)
                t = tt(c[11], c[11], c[12], SUB, t)
                t = tt(qim, c[11], c[10], MUL, t)
                big = ROUND / 4096.0
                t = ts(c[13], ph, big, big, ADD, SUB, t)
                t = tt(c[14], ph, c[13], SUB, t)
                for n in range(8):
                    t = ts(w[:, n, :], C("iota"), c[13][:, n:n + 1], None, MUL, None, t)
                t = round_off(w[:, :, :], tmp[:, :, :], t)
                for n in range(8):
                    t = stt(w[:, n, :], C("iota"), c[14][:, n:n + 1], w[:, n, :], MUL, ADD, t)
                t = round_off(w[:, :, :], tmp[:, :, :], t)
                t1 = act(sinT[:, :, :], w[:, :, :], ACT.Sin, t, scale=6.283185)
                t = ts(w[:, :, :], w[:, :, :], 0.25, None, ADD, None, t1)
                t = round_off(w[:, :, :], tmp[:, :, :], t)
                t1 = act(cosT[:, :, :], w[:, :, :], ACT.Sin, t, scale=6.283185)
                V.wait(t1)
                return t1

        def modulation():
            sc = s5p[:, 15, :]
            t = act(sc, P("c", 0, 8), ACT.Sigmoid)
            t = tt(sc, sc, P("c", 0, 8), MUL, t)
            b, p = bank()
            for m in range(48):
                t1 = linear(d["ada_w"], m, lambda k: sc[:, k:k + 1], 8, p[:, m:m + 1], [t])
            t = tt(mod[:, :], p[:, 0:48], P("ada_b", 0, 48), ADD, t1)
            done(b, t)
            for n, nm in enumerate(("norm_mix2", "norm_ffn2")):
                t = stt(gsc[:, n, :], mod[:, 24 * n + 8:24 * n + 16], 1.0, P(nm, 0, 8), ADD, MUL, t)
            return t

        def mod_norm(n, t_x, t_m):
            t = norm_stats(t_x)
            r = rst[:, :].unsqueeze(1).to_broadcast([128, 8, T])
            t = tt(h[:, :, :], x[:, :, :], r, MUL, t)
            for k in range(8):
                t1 = act(h[:, k, :], h[:, k, :], ACT.Identity, t, t_m, scale=gsc[:, n, k:k + 1],
                         bias=mod[:, 24 * n + k:24 * n + k + 1])
            return t1

        def mixers(t_x, t_m):
            t_h = mod_norm(0, t_x, t_m)
            W = d["w_in"]
            with ExitStack() as st:
                gates = alloc(st, "gates", [128, 32, T])
                yin = alloc(st, "yin", [128, 8, T])
                lora = alloc(st, "lora", [128, 256])
                s_l = sem("s_lora")
                for q in (V, A, G):
                    q.wait(t_h)
                A.dma(lora[:, :], d["lora"], s_l, t_h)
                t_l = (s_l, 16)

                def proj(m, use):
                    b, p = bank()
                    t = linear(W, m, hk, 8, p[:, 0:T], [t_h])
                    t = use(p[:, 0:T], t)
                    done(b, t)
                    return t

                def rwkv():
                    s2 = ExitStack()
                    al = lambda n, sh: alloc(s2, n, sh)
                    f = {n: al(n, [128, 2, T]) for n in ("r", "k", "v", "b", "ks", "at", "rt", "bn", "g", "e")}
                    lo = al("lo", [128, T])
                    omu = al("omu", [128, 8])
                    t_o = ts(omu[:, 0:7], P("mu", 0, 7), -1.0, 1.0, MUL, ADD)
                    t_o = ts(omu[:, 7:8], P("mu", 0, 1), 0.0, None, MUL, None)

                    def shift(o, m):
                        def use(p, t):
                            t = act(o, p, ACT.Copy, t, t_o, scale=omu[:, m:m + 1])
                            return stt(o[:, 1:], p[:, 0:T - 1], P("mu", m), o[:, 1:], MUL, ADD, t)
                        return proj(m, use)

                    t_lo = shift(lo[:, :], 6)
                    tk = [shift(f["k"][:, j, :], 2 + j) for j in range(2)]
                    tr = [shift(f["r"][:, j, :], j) for j in range(2)]
                    tv = [shift(f["v"][:, j, :], 4 + j) for j in range(2)]
                    yield
                    t1 = act(lo[0:32, :], lo[0:32, :], ACT.Tanh, t_lo)
                    t2 = act(lo[64:128, :], lo[64:128, :], ACT.Sigmoid, t_lo)
                    ld, e = al("ld", [128, 2, T]), f["e"]
                    aa = al("aa", [128, 2, T])
                    b, p = bank()
                    b2, p2 = bank()
                    b3, p3 = bank()
                    for j in range(2):
                        c, o = slice(j * 128, j * 128 + 128), slice(j * T, j * T + T)
                        ta = mm(p[:, o], lora[0:32, c], lo[0:32, :], t1, t2, t_l)
                        tb = mm(p2[:, o], lora[32:64, c], lo[32:64, :])
                        tc = mm(p3[:, o], lora[64:128, c], lo[64:128, :])
                    for j in range(2):
                        o = slice(j * T, j * T + T)
                        ta = act(ld[:, j, :], p[:, o], ACT.Sigmoid, tc, bias=P("w0", j))
                        tb = act(aa[:, j, :], p2[:, o], ACT.Sigmoid, tb, bias=P("a0", j))
                        tc = copy(f["g"][:, j, :], p3[:, o], tc, q=A)
                    done(b, ta)
                    done(b2, tb)
                    done(b3, tc)
                    yield
                    t_ld = ts(ld[:, :, :], ld[:, :, :], -0.6065306597126334, None, MUL, None, ta)
                    cs, mid, en = al("cs", [128, 2, T]), al("mid", [128, 8]), al("en", [128, 8])
                    for j in range(2):
                        t = V.run(lambda e_, j=j: e_.tensor_tensor_scan(cs[:, j, :], C("smask"), ld[:, j, :], 0.0, MUL, ADD), t_ld)
                    c4 = cs[:, :, :].rearrange("p j (c t) -> p (j c) t", t=64)
                    t = copy(mid[:, :].unsqueeze(2), c4[:, :, 31:32], t)
                    t = tt(c4, c4, mid[:, :].unsqueeze(2).to_broadcast([128, 8, 64]), SUB, t)
                    t_c = t
                    t = copy(en[:, :].unsqueeze(2), c4[:, :, 63:64], t)
                    m4, e4 = mid[:, :].rearrange("p (j c) -> p j c", j=2), en[:, :].rearrange("p (j c) -> p j c", j=2)
                    t = tt(e4[:, :, 0:3], e4[:, :, 0:3], m4[:, :, 1:4], ADD, t)
                    t_f = act(en[:, :], en[:, :], ACT.Exp, t)
                    t = tt(ld[:, :, :], cs[:, :, :], ld[:, :, :], SUB, t_c)
                    t_e1 = act(f["rt"][:, :, :], cs[:, :, :], ACT.Exp, t_c)
                    t_e2 = act(cs[:, :, :], cs[:, :, :], ACT.Exp, t_e1, t, scale=-1.0)
                    t_e3 = act(ld[:, :, :], ld[:, :, :], ACT.Exp, t)
                    yield
                    kh, b_ = f["at"], f["b"]
                    for j in range(2):
                        t = ts(kh[:, j, :], f["k"][:, j, :], P("kk", j), None, MUL, None, tk[j])
                    t = tt(e[:, :, :], kh[:, :, :], kh[:, :, :], MUL, t)
                    b, p = bank()
                    t = mm(p[:, 0:512], blk, e[:, :, :], t)
                    yield
                    t = act(e[:, :, :], p[:, 0:512].rearrange("p (j t) -> p j t", j=2), ACT.Sqrt, t)
                    done(b, t)
                    t = ts(e[:, :, :], e[:, :, :], 1e-12, None, MAX, None, t)
                    t = recip(e[:, :, :], e[:, :, :], t)
                    t = tt(kh[:, :, :], kh[:, :, :], e[:, :, :], MUL, t)
                    t = tt(b_[:, :, :], kh[:, :, :], aa[:, :, :], MUL, t, tb)
                    for j in range(2):
                        t1 = ts(aa[:, j, :], aa[:, j, :], 1.0, P("ka", j), SUB, MUL, t)
                    t1 = stt(f["k"][:, :, :], aa[:, :, :], 1.0, f["k"][:, :, :], ADD, MUL, t1)
                    for j in range(2):
                        t2 = stt(e[:, j, :], f["r"][:, j, :], P("rk", j), f["k"][:, j, :], MUL, MUL, t1, tr[j])
                    b, p = bank()
                    t2 = mm(p[:, 0:512], blk, e[:, :, :], t2)
                    yield
                    t_bn = tt(f["bn"][:, :, :], p[:, 0:512].rearrange("p (j t) -> p j t", j=2), f["v"][:, :, :], MUL, t2, tv)
                    done(b, t_bn)
                    t = stt(kh[:, :, :], kh[:, :, :], -1.0, ld[:, :, :], MUL, MUL, t_e3, t)
                    t = tt(f["rt"][:, :, :], f["rt"][:, :, :], f["r"][:, :, :], MUL, t_e1)
                    t = tt(b_[:, :, :], b_[:, :, :], cs[:, :, :], MUL, t_e2)
                    t_s = tt(f["ks"][:, :, :], f["k"][:, :, :], cs[:, :, :], MUL, t_e2)
                    At, Rt, Bs, Ks = f["at"], f["rt"], f["b"], f["ks"]
                    BT, KT, VT = (al(n, [128, 2, 256]) for n in ("BT", "KT", "VT"))
                    t_tr = {}
                    for nm, src, dst in (("b", Bs, BT), ("k", Ks, KT), ("v", f["v"], VT)):
                        b, p = bank()
                        for z in range(2):
                            for j in range(2):
                                t = PE.run(lambda e_, p=p, z=z, j=j, src=src: e_.transpose(
                                    p[:, (2 * z + j) * 128:(2 * z + j + 1) * 128],
                                    src[:, j, z * 128:(z + 1) * 128], ident), t_s, tv)
                        t = copy(dst[:, :, :], p[:, 0:512].rearrange("p (z c) -> p z c", z=2), t, q=A)
                        done(b, t)
                        t_tr[nm] = t
                    yield
                    N, NR, MK, MR, X, Y, Q, NL = (al(n, [128, 2, 4, 128]) for n in ("N", "NR", "MK", "MR", "X", "Y", "Q", "NL"))

                    def bc(name):
                        return C(name).unsqueeze(1).to_broadcast([128, 4, 128])

                    tn, tmk, tnr, t_xy = [None] * 2, [None] * 2, [None] * 2, [None] * 2
                    for z in range(2):
                        zs = slice(z * 128, z * 128 + 128)
                        for dst, l, r, mk in ((N, Bs, At, "su"), (NR, Bs, Rt, "iu"), (MK, Ks, At, "su"), (MR, Ks, Rt, "iu"), (NL, At, Bs, "l0t")):
                            b, p = bank()
                            for hd in (0, 2, 1, 3):
                                j, r0 = hd // 2, 64 * (hd % 2)
                                t = mm(p[:, hd * 128:hd * 128 + 128], l[r0:r0 + 64, j, zs], r[r0:r0 + 64, j, zs],
                                       t if hd == 1 else t_s)
                            t = tt(dst[:, z, :, :], p[:, :].rearrange("p (h t) -> p h t", h=4), bc(mk), MUL, t)
                            done(b, t)
                        t = tt(Y[:, z, :, :], NL[:, z, :, :], bc("ident"), ADD, t)
                        t2 = tt(X[:, z, :, :], N[:, z, :, :], bc("l0"), MUL, t)
                        t_xy[z] = tt(X[:, z, :, :], X[:, z, :, :], bc("ident"), ADD, t2)
                        yield
                    for lv in range(1, 6):
                        for z in range(2):
                            t = tt(NL[:, z, :, :], N[:, z, :, :], bc(f"l{lv}"), MUL, t_xy[z])
                            b, p = bank()
                            for hd in range(4):
                                t1 = mm(p[:, hd * 128:hd * 128 + 128], NL[:, z, hd, :], Y[:, z, hd, :], t)
                            t1 = copy(Q[:, z, :, :], p[:, :].rearrange("p (h t) -> p h t", h=4), t1, q=A)
                            done(b, t1)
                            t_xy[z] = t1
                        yield
                        for z in range(2):
                            t1 = t_xy[z]
                            b, p = bank()
                            for hd in range(4):
                                t2 = mm(p[:, hd * 128:hd * 128 + 128], Q[:, z, hd, :], X[:, z, hd, :], t1)
                            if lv < 5:
                                b3, p3 = bank()
                                for hd in range(4):
                                    t2 = mm(p3[:, hd * 128:hd * 128 + 128], X[:, z, hd, :], Q[:, z, hd, :])
                            t = tt(X[:, z, :, :], p[:, :].rearrange("p (h t) -> p h t", h=4), X[:, z, :, :], ADD, t2)
                            done(b, t)
                            if lv < 5:
                                t = tt(Y[:, z, :, :], p3[:, :].rearrange("p (h t) -> p h t", h=4), Y[:, z, :, :], ADD, t2)
                                done(b3, t)
                            t_xy[z] = t
                        yield
                    U0, SA, R = (al(n, [128, 2, 256]) for n in ("U0", "SA", "R"))
                    S0 = al("S0", [128, 4, 2, 128])
                    for z in range(2):
                        b, p = bank()
                        for hd in range(4):
                            t = mm(p[:, hd * 64:hd * 64 + 64], MK[:, z, hd, :], VT[:, z, hd * 64:hd * 64 + 64], t_xy[z], t_tr["v"])
                        t = copy(U0[:, z, :], p[:, 0:256], t, q=A)
                        done(b, t)
                    t_u = t
                    t_s0 = V.run(lambda e_: e_.memset(S0[:, 0, :, :], 0.0))
                    yield
                    for c in range(4):
                        z, q0 = c // 2, 64 * (c % 2)
                        rows = slice(q0, q0 + 64)
                        b, p = bank()
                        for j in range(2):
                            t = mm(p[:, j * 128:j * 128 + 128], At[:, j, z * 128:z * 128 + 128], S0[:, c, j, :], t_s0)
                        t = tt(R[rows, z, :], p[rows, 0:256], U0[rows, z, :], ADD, t, t_u)
                        done(b, t)
                        yield
                        b, p = bank()
                        for hd in range(4):
                            t2 = mm(p[rows, hd * 64:hd * 64 + 64], X[rows, z, hd, rows], R[rows, z, hd * 64:hd * 64 + 64], t)
                        t_sa = copy(SA[rows, z, :], p[rows, 0:256], t2, q=A)
                        done(b, t_sa)
                        if c == 3:
                            break
                        yield
                        b, p = bank()
                        for j in range(2):
                            js = slice(j * 128, j * 128 + 128)
                            mm(p[:, js], KT[rows, z, js], VT[rows, z, js], t_tr["k"], t_tr["b"], stop=False, last=False)
                            t = mm(p[:, js], BT[rows, z, js], SA[rows, z, js], t_sa, start=False)
                        nx = S0[:, c + 1, :, :]
                        t = tt(nx, p[:, 0:256].rearrange("p (j i) -> p j i", j=2), C("blk").unsqueeze(1).to_broadcast([128, 2, 128]), MUL, t)
                        done(b, t)
                        t = tt(nx, nx, S0[:, c, :, :], ADD, t)
                        for j in range(2):
                            t_s0 = ts(S0[:, c + 1, j, :], S0[:, c + 1, j, :], en[:, 4 * j + c:4 * j + c + 1], None, MUL, None, t, t_f)
                        yield
                    o_ = f["k"]
                    for j in range(2):
                        b, p = bank()
                        for u in range(2):
                            hd, r0 = 2 * j + u, 64 * u
                            for z in range(2):
                                o = p[r0:r0 + 64, z * 128:z * 128 + 128]
                                mm(o, SA[:, z, hd * 64:hd * 64 + 64], NR[:, z, hd, :], t_sa, last=False, stop=False)
                                mm(o, VT[:, z, hd * 64:hd * 64 + 64], MR[:, z, hd, :], last=False, stop=False, start=False)
                                for y in range(2):
                                    c = 2 * z + y
                                    t = mm(p[r0:r0 + 64, c * 64:c * 64 + 64], S0[:, c, j, r0:r0 + 64], Rt[:, j, c * 64:c * 64 + 64],
                                           t_s0, start=False, stop=y == 1)
                        t = copy(o_[:, j, :], p[:, 0:T], t, q=A)
                        done(b, t)
                    dump("o", o_[:, :, :], t)
                    yield
                    b, p = bank()
                    t1 = mm(p[:, :], blk, o_[:, :, :], t)
                    yield
                    p_ = p[:, :].rearrange("p (j t) -> p j t", j=2)
                    t = stt(o_[:, :, :], p_, -1.0 / 64, o_[:, :, :], MUL, ADD, t1)
                    done(b, t)
                    t1 = tt(e[:, :, :], o_[:, :, :], o_[:, :, :], MUL, t)
                    b, p = bank()
                    t1 = mm(p[:, :], blk, e[:, :, :], t1)
                    yield
                    p_ = p[:, :].rearrange("p (j t) -> p j t", j=2)
                    t1 = ts(e[:, :, :], p_, 1.0 / 64, 64e-5, MUL, ADD, t1)
                    done(b, t1)
                    t1 = act(e[:, :, :], e[:, :, :], ACT.Sqrt, t1)
                    t1 = recip(e[:, :, :], e[:, :, :], t1)
                    for j in range(2):
                        t = stt(o_[:, j, :], o_[:, j, :], P("lnw", j), e[:, j, :], MUL, MUL, t1)
                        t = stt(o_[:, j, :], o_[:, j, :], P("lnb", j), f["bn"][:, j, :], ADD, ADD, t)
                    t = tt(yin[:, 0:2, :], o_[:, :, :], f["g"][:, :, :], MUL, t)
                    dump("ya", yin[:, 0:2, :], t)
                    toks["a"] = t
                    s2.close()

                def s5():
                    s2 = ExitStack()
                    al = lambda n, sh: alloc(s2, n, sh)
                    u = al("su", [128, 2, T])
                    bd = al("bd", [128, 2, 2, 64])
                    bp = al("bp", [128, 2, 2, 8, 64])
                    cd = al("cd", [128, 2, 8, 16])
                    cc = al("cc", [128, 2, 8, 16])
                    cp = al("cp", [128, 2, 8, 128])
                    s_b = sem("s_s5")
                    gate_ = (V.sem, V.n)
                    A.dma(bd[:, :, :, :], d["s5b"], s_b, gate_, (PE.sem, PE.n), (G.sem, G.n))
                    A.dma(cd[:, :, :, :], d["s5c"], s_b)
                    t_b = (s_b, 32)
                    tu = [proj(17 + j, lambda p, t, j=j: copy(u[:, j, :], p, t, q=A)) for j in range(2)]
                    yield
                    bm = C("bmask").unsqueeze(2).to_broadcast([128, 8, 64])
                    for ri in range(2):
                        for hf in range(2):
                            t = tt(bp[:, ri, hf, :, :], bd[:, ri, hf, :].unsqueeze(1).to_broadcast([128, 8, 64]), bm, MUL, t_b)
                    t_bp = t
                    qre = s5p[:, 4, :].unsqueeze(2).to_broadcast([128, 8, 16])
                    qim = s5p[:, 5, :].unsqueeze(2).to_broadcast([128, 8, 16])
                    cr, ci = cd[:, 0, :, :], cd[:, 1, :, :]
                    t = tt(cc[:, 0, :, :], cr, qre, MUL, t_b)
                    t1 = tt(cc[:, 1, :, :], ci, qim, MUL, t_b)
                    t = tt(cc[:, 0, :, :], cc[:, 0, :, :], cc[:, 1, :, :], SUB, t, t1)
                    t1 = tt(cc[:, 1, :, :], cr, qim, MUL, t)
                    t2 = tt(cd[:, 0, :, :], ci, qre, MUL, t1)
                    t1 = stt(cc[:, 1, :, :], cc[:, 1, :, :], -1.0, cd[:, 0, :, :], MUL, SUB, t1, t2)
                    cm = C("cmask").rearrange("p (j g) -> p j g", j=4)
                    for ri in range(2):
                        for i in range(8):
                            m = cm[:, i % 4, :].unsqueeze(2).to_broadcast([128, 8, 16])
                            s = cc[:, ri, i, :].unsqueeze(1).to_broadcast([128, 8, 16])
                            t = tt(cp[:, ri, i, :].rearrange("p (g c) -> p g c", g=8), s, m, MUL, t, t1)
                    t_cp = t
                    yield
                    z = al("z", [128, 2, 8, T])
                    w = al("sw", [128, 2, 6, T])
                    old = [None, None]
                    for i in range(8):
                        hf = i // 4
                        co, si = cosT[:, i, :], sinT[:, i, :]
                        b, p = bank()
                        b2, p2 = bank()
                        t = mm(p[:, 0:T], bp[:, 0, hf, 2 * (i % 4):2 * (i % 4) + 2, :], u[:, hf, :], t_bp, tu[hf])
                        t2 = mm(p2[:, 0:T], bp[:, 1, hf, 2 * (i % 4):2 * (i % 4) + 2, :], u[:, hf, :])
                        w_ = [w[:, i % 2, n, :] for n in range(6)]
                        ta = tt(w_[0], p[:, 0:T], co, MUL, t, old[i % 2])
                        tb = tt(w_[3], p[:, 0:T], si, MUL, t)
                        done(b, tb)
                        tc = tt(w_[1], p2[:, 0:T], si, MUL, t2)
                        td = tt(w_[2], p2[:, 0:T], co, MUL, t2)
                        done(b2, td)
                        ta = tt(w_[0], w_[0], w_[1], ADD, tc)
                        tb = tt(w_[2], w_[2], w_[3], SUB, td)
                        mg = s5p[:, 2, i:i + 1].to_broadcast([128, T])
                        ta = V.run(lambda e, w_=w_, mg=mg: e.tensor_tensor_scan(w_[4], mg, w_[0], 0.0, MUL, ADD), ta)
                        tb = V.run(lambda e, w_=w_, mg=mg: e.tensor_tensor_scan(w_[5], mg, w_[2], 0.0, MUL, ADD), tb)
                        ta = tt(w_[0], w_[4], co, MUL, ta, tb, q=G)
                        tb = tt(w_[1], w_[5], si, MUL, tb, q=G)
                        tc = tt(w_[2], w_[5], co, MUL, q=G)
                        td = tt(w_[3], w_[4], si, MUL, q=G)
                        ta = tt(z[:, 0, i, :], w_[0], w_[1], SUB, ta, tb, q=G)
                        tb = tt(z[:, 1, i, :], w_[2], w_[3], ADD, tc, td, q=G)
                        old[i % 2] = tb
                        yield
                    for hf in range(2):
                        b, p = bank()
                        n = 0
                        for i in range(4 * hf, 4 * hf + 4):
                            for ri in range(2):
                                t = mm(p[:, 0:T], cp[:, ri, i, :], z[:, ri, i, :], t_cp, tb, start=n == 0, stop=n == 7)
                                n += 1
                        t = stt(u[:, hf, :], u[:, hf, :], P("s_d", hf), p[:, 0:T], MUL, ADD, t)
                        done(b, t)
                        t = act(yin[:, 6 + hf, :], u[:, hf, :], ACT.Gelu_apprx_tanh, t)
                    dump("yd", yin[:, 6:8, :], t)
                    toks["d"] = t
                    s2.close()

                def sg():
                    s2 = ExitStack()
                    al = lambda n, sh: alloc(s2, n, sh)
                    gu = al("gu", [128, 2, T])
                    gv = al("gv", [128, 2, T])
                    e = al("ge", [128, 2, T])
                    me = al("me", [128, T])
                    ws = al("ws", [128, 4, 128])
                    bs_ = al("bs", [128, 2, 128])
                    vT = al("gvT", [128, 2, 256])
                    s_g = sem("s_sg")
                    A.dma(ws[:, :, :], d["sg_ws"], s_g, (V.sem, V.n), (PE.sem, PE.n), (G.sem, G.n))
                    A.dma(bs_[:, :, :], d["sg_bs"], s_g)
                    tu = [proj(7 + j, lambda p, t, j=j: act(gu[:, j, :], p, ACT.Gelu_apprx_tanh, t)) for j in range(2)]
                    tv = [proj(9 + j, lambda p, t, j=j: act(gv[:, j, :], p, ACT.Gelu_apprx_tanh, t)) for j in range(2)]
                    yield
                    t_w = tt(ws[:, :, :], ws[:, :, :], C("sgm").unsqueeze(1).to_broadcast([128, 4, 128]), MUL, (s_g, 32))
                    b, p = bank()
                    for j in range(2):
                        t = mm(p[:, 0:T], ones, gv[:, j, :], tv[j], start=j == 0, stop=j == 1)
                    t = ts(me[:, :], p[:, 0:T], 1.0 / 256, None, MUL, None, t)
                    done(b, t)
                    t = tt(gv[:, :, :], gv[:, :, :], me[:, :].unsqueeze(1).to_broadcast([128, 2, T]), SUB, t)
                    t1 = tt(e[:, :, :], gv[:, :, :], gv[:, :, :], MUL, t)
                    yield
                    b, p = bank()
                    for j in range(2):
                        t = mm(p[:, 0:T], ones, e[:, j, :], t1, start=j == 0, stop=j == 1)
                    t = ts(me[:, :], p[:, 0:T], 1.0 / 256, 1e-5, MUL, ADD, t)
                    done(b, t)
                    t = act(me[:, :], me[:, :], ACT.Sqrt, t)
                    t = recip(me[:, :], me[:, :], t)
                    for j in range(2):
                        t1 = stt(gv[:, j, :], gv[:, j, :], P("sglw", j), me[:, :], MUL, MUL, t)
                        t1 = ts(gv[:, j, :], gv[:, j, :], P("sglb", j), None, ADD, None, t1)
                    yield
                    b, p = bank()
                    for z in range(2):
                        for j in range(2):
                            t = PE.run(lambda e_, p=p, z=z, j=j: e_.transpose(
                                p[:, (2 * z + j) * 128:(2 * z + j + 1) * 128], gv[:, j, z * 128:z * 128 + 128], ident), t1)
                    t = copy(vT[:, :, :], p[:, :].rearrange("p (z c) -> p z c", z=2), t, q=A)
                    done(b, t)
                    yield
                    for j in range(2):
                        b, p = bank()
                        for u in range(2):
                            g = 2 * j + u
                            for z in range(2):
                                t1 = mm(p[64 * u:64 * u + 64, z * 128:z * 128 + 128], vT[:, z, g * 64:g * 64 + 64], ws[:, g, :], t, t_w)
                        t1 = tt(e[:, j, :].rearrange("p (z t) -> p z t", z=2), p[:, 0:T].rearrange("p (z t) -> p z t", z=2),
                                bs_[:, j, :].unsqueeze(1).to_broadcast([128, 2, 128]), ADD, t1)
                        done(b, t1)
                    t = tt(yin[:, 2:4, :], e[:, :, :], gu[:, :, :], MUL, t1, tu[1])
                    dump("yb", yin[:, 2:4, :], t)
                    toks["b"] = t
                    s2.close()

                def sconv():
                    s2 = ExitStack()
                    al = lambda n, sh: alloc(s2, n, sh)
                    c = {n: al("c" + n, [128, 2, T]) for n in ("b", "c", "y")}
                    V.wait((PE.sem, PE.n), (G.sem, G.n))
                    A.wait((V.sem, V.n), (PE.sem, PE.n), (G.sem, G.n))
                    tb = [proj(11 + j, lambda p, t, j=j: copy(c["b"][:, j, :], p, t, q=A)) for j in range(2)]
                    tc = [proj(13 + j, lambda p, t, j=j: copy(c["c"][:, j, :], p, t, q=A)) for j in range(2)]
                    for j in range(2):
                        ci = c["c"][:, j, :]
                        t = proj(15 + j, lambda p, t, ci=ci, j=j: tt(ci, p, ci, MUL, t, tc[j]))
                        t = conv_taps(c["y"][:, j, :], ci, "cw", 2, j, 3, t, 0.0)
                        t = tt(yin[:, 4 + j, :], c["y"][:, j, :], c["b"][:, j, :], MUL, t, tb[j])
                    dump("yc", yin[:, 4:6, :], t)
                    toks["c"] = t
                    s2.close()
                    return
                    yield

                toks = {}
                tgs = [None] * 32
                gi = [0]

                def gate_tile():
                    m = gi[0]
                    if m >= 32:
                        return
                    gi[0] += 1
                    tgs[m] = proj(19 + m, lambda p, t: copy(gates[:, m, :], p, t, q=(A, V)[m % 2]))

                for part in (sconv, sg, s5, rwkv):
                    first = True
                    for q in (V, A, G):
                        q.wait((PE.sem, PE.n), (V.sem, V.n), (A.sem, A.n), (G.sem, G.n))
                    for _ in part():
                        if not first and part is rwkv:
                            gate_tile()
                        first = False
                while gi[0] < 32:
                    gate_tile()
                h_free[0] = (PE.sem, PE.n)
                t_h2 = h_free[0]
                t_y = [toks[n] for n in "abcd"]
                scr = alloc(st, "scr", [128, 8, T])
                for q in (V, A):
                    q.wait((PE.sem, PE.n), (V.sem, V.n), (A.sem, A.n), (G.sem, G.n))
                g4 = gates[:, :, :].rearrange("p (n m) t -> p m n t", n=4)
                old = [None, None]
                for m in range(8):
                    tg = act(g4[:, m, :, :], g4[:, m, :, :], ACT.Sigmoid, tgs[m], tgs[8 + m], tgs[16 + m], tgs[24 + m])
                    w = [scr[:, 4 * (m % 2) + n, :] for n in range(4)]
                    i1, tok1 = load(d["yw"][m, :, 0:5, :], 5)
                    i2, tok2 = load(d["yw"][m, :, 5:10, :], 5)
                    outs = []
                    for n in range(5):
                        if n == 3:
                            bb, pp = bank()
                        o = None
                        if n < 3:
                            b, p = bank()
                            o = p[:, 0:T]
                            outs.append((b, o))
                        else:
                            o = pp[:, (n - 3) * T:(n - 2) * T]
                        for k in range(2):
                            q = 2 * n + k
                            i, q_ = (i1, q) if q < 5 else (i2, q - 5)
                            t = mm(o, ring[i][:, q_, :], yin[:, 2 * min(n, 3) + k, :], tok1, tok2, t_y, start=k == 0, stop=k == 1)
                            if n < 3:
                                outs[n] = (b, o, t)
                    rfree[i1] = rfree[i2] = t
                    ts_ = act(w[3], pp[:, T:2 * T], ACT.Sigmoid, t, old[m % 2])
                    t3 = tt(w[3], pp[:, 0:T], w[3], MUL, ts_)
                    done(bb, t3)
                    t3 = tt(w[3], w[3], gates[:, 24 + m, :], MUL, t3, tg)
                    tn = []
                    for n in range(3):
                        b, o, t = outs[n]
                        t = tt(w[n], o, gates[:, 8 * n + m, :], MUL, t, tg)
                        done(b, t)
                    ta = tt(w[0], w[0], w[1], ADD, t)
                    tb = tt(w[2], w[2], w[3], ADD, t3, t)
                    old[m % 2] = tt(h[:, m, :], w[0], w[2], ADD, ta, tb, t_h2)
                dump("merged", h[:, :, :], old[1])
                t = residual(d["w_o"], 8, hk, [old[1]], scale=lambda m: mod[:, 16 + m:17 + m])
                h_free[0] = (PE.sem, PE.n)
                return t

        def relu_ffn(t_x, t_m):
            t_h = mod_norm(1, t_x, t_m)
            with ExitStack() as st:
                hid = alloc(st, "hid2", [128, 32, T])
                for q in (V, A):
                    q.wait(t_h)
                for m in range(32):
                    b, p = bank()
                    t = linear(d["ffn_w1"], m, hk, 8, p[:, 0:T], [t_h])
                    t = act(hid[:, m, :], p[:, 0:T], ACT.Relu, t)
                    done(b, t)
                    t = tt(hid[:, m, :], hid[:, m, :], hid[:, m, :], MUL, t)
                h_free[0] = (PE.sem, PE.n)
                return residual(d["ffn_w2"], 32, lambda k: hid[:, k, :], [t], scale=lambda m: mod[:, 40 + m:41 + m])

        t = pool_attn(t_x)
        dump("x1", x[:, :, :], t)
        t_s5 = s5_params()
        t = conv_ffn(0, t)
        dump("x2", x[:, :, :], t)
        t = rglru(t)
        dump("x3", x[:, :, :], t)
        t = conv_ffn(1, t)
        dump("x4", x[:, :, :], t)
        t_m = modulation()
        t = mixers(t, t_m)
        dump("x5", x[:, :, :], t)
        t = relu_ffn(t, t_m)
        dump("x6", x[:, :, :], t)
        t = norm("final_g", t)
        s_out = sem("s_out")
        SP.dma(out, h[:, :, :], s_out, t)
        SP.wait((s_out, 16))
        SP.wait(*dbgs)

        with nc.Block() as block:
            @block.sync
            def _(e):
                SP.play(e)

            @block.scalar
            def _(e):
                A.play(e)

            @block.vector
            def _(e):
                V.play(e)

            @block.gpsimd
            def _(e):
                G.play(e)

            @block.tensor
            def _(e):
                PE.play(e)


def lay(i):
    a = {k: np.asarray(v) for k, v in i.items()}

    def tiles(w):
        k, m = w.shape
        return np.ascontiguousarray(w.reshape(k // 128, 128, m // 128, 128).transpose(2, 1, 0, 3))

    def cols(v):
        return v.reshape(-1, 128).T

    o = {}
    o["xT"] = a["x"][0].T.reshape(8, 128, 256).transpose(1, 0, 2)
    o["cst"] = const_array()
    v = {
        "norm_mix0": a["norm_mix"][0], "norm_mix1": a["norm_mix"][1], "norm_ffn0": a["norm_ffn"][0],
        "norm_ffn1": a["norm_ffn"][1], "pool_scale": a["pa_pool_scale"][0],
        "q_gain": np.concatenate([a["pa_q_gain"][0]] * 2), "k_gain": np.concatenate([a["pa_k_gain"][0]] * 2),
        "rg_cw": a["rg_conv_w"][0], "rg_cb": a["rg_conv_b"][0], "rg_ba": a["rg_b_a"][0], "rg_bx": a["rg_b_x"][0],
        "rg_lam": a["rg_lambda"][0], "ffn_cw0": a["ffn_conv_w"][0], "ffn_cw1": a["ffn_conv_w"][1],
        "ffn_cb0": a["ffn_conv_b"][0], "ffn_cb1": a["ffn_conv_b"][1], "c": a["c_2"], "ada_b": a["ada_b_2"],
        "norm_mix2": a["norm_mix_g_2"], "mu": a["rwkv_mu_2"], "w0": a["rwkv_w0_2"], "a0": a["rwkv_a0_2"],
        "kk": a["rwkv_kk_2"], "ka": a["rwkv_ka_2"], "rk": a["rwkv_rk_2"], "lnw": a["rwkv_lnx_w_2"],
        "lnb": a["rwkv_lnx_b_2"], "sglw": a["sg_ln_w_2"], "sglb": a["sg_ln_b_2"], "cw": a["conv_w_2"],
        "s_are": a["s5_a_re_2"], "s_aim": a["s5_a_im_2"], "s_ldt": np.repeat(a["s5_log_dt_2"].reshape(16), 64),
        "s_d": a["s5_d_2"], "norm_ffn2": a["norm_ffn_g_2"], "final_g": a["final_g_2"],
    }
    o["vec"] = np.concatenate([cols(v[n]) for n, _ in VECS], 1)
    o["pa_w_in"] = tiles(a["pa_w_in"][0])
    o["pool_w"] = a["pa_pool_w"][0].transpose(1, 0, 2)
    o["pa_w_out"] = tiles(a["pa_w_out"][0])
    o["rg_w_in"] = tiles(a["rg_w_in"][0])
    o["rg_wab"] = np.concatenate([a["rg_w_a"][0], a["rg_w_x"][0]], 0).transpose(1, 0, 2)
    o["rg_w_out"] = tiles(a["rg_w_out"][0])
    for l in range(2):
        o[f"ffn_w_in{l}"] = tiles(a["ffn_w_in"][l])
        o[f"ffn_w_out{l}"] = tiles(a["ffn_w_out"][l])
    o["ada_w"] = tiles(a["ada_w_2"][0])
    o["w_in"] = tiles(a["w_in_2"][0])
    o["lora"] = np.concatenate([a["rwkv_w2_2"][0], a["rwkv_a2_2"][0], a["rwkv_g2_2"][0]], 0)
    glu = tiles(a["s5_glu_w_2"][0])
    o["yw"] = np.concatenate([tiles(a["rwkv_out_2"][0]), tiles(a["sg_out_2"][0]), tiles(a["conv_out_2"][0]),
                              glu[:8], glu[8:]], 2)
    o["sg_ws"] = a["sg_ws_2"][0].transpose(2, 0, 1)
    o["sg_bs"] = np.repeat(a["sg_bs_2"][0], 64, 0).reshape(2, 128, 128).transpose(1, 0, 2)
    sb = np.stack([a["s5_b_re_2"][0], a["s5_b_im_2"][0]]).reshape(2, 2, 8, 64, 16)
    o["s5b"] = sb.transpose(2, 4, 0, 1, 3).reshape(128, 2, 2, 64)
    sc = np.stack([a["s5_c_re_2"][0], a["s5_c_im_2"][0]]).reshape(2, 8, 2, 16, 64)
    o["s5c"] = sc.transpose(2, 4, 0, 1, 3).reshape(128, 2, 8, 16)
    o["w_o"] = tiles(a["w_o_2"][0])
    o["ffn_w1"] = tiles(a["ffn_w1_2"][0])
    o["ffn_w2"] = tiles(a["ffn_w2_2"][0])
    return {k: np.ascontiguousarray(w) for k, w in o.items()}


def kernel(**inputs):
    import concourse.bacc as bacc
    from concourse.bass_utils import run_bass_kernel_spmd

    arrays = lay(inputs)
    nc = bacc.Bacc("TRN2", target_bir_lowering=False, num_devices=1)
    d = {n: nc.dram_tensor(n, a.shape, F32, kind="ExternalInput").ap() for n, a in arrays.items()}
    out = nc.dram_tensor("out", (128, 8, 256), F32, kind="ExternalOutput").ap()
    build(nc, d, out)
    r = run_bass_kernel_spmd(nc, [arrays], core_ids=[0])
    o = r.results[0]["out"]
    return o.transpose(1, 0, 2).reshape(1024, 256).T.reshape(1, 256, 1024)
```

```python
from contextlib import ExitStack

import concourse.bass as bass
import numpy as np
from concourse import mybir

F32 = mybir.dt.float32
F32R = mybir.dt.float32r
ALU = mybir.AluOpType
ACT = mybir.ActivationFunctionType
AX = mybir.AxisListType.X
NEG = mybir.AluOpType.subtract
T = 256
TWO_PI = 6.283185307179586
ROUND = 12582912.0

VECS = [
    ("norm_mix0", 8), ("norm_mix1", 8), ("norm_ffn0", 8), ("norm_ffn1", 8), ("pool_scale", 4),
    ("q_gain", 1), ("k_gain", 1), ("rg_cw", 40), ("rg_cb", 10), ("rg_ba", 10), ("rg_bx", 10),
    ("rg_lam", 10), ("ffn_cw0", 132), ("ffn_cw1", 132), ("ffn_cb0", 44), ("ffn_cb1", 44),
    ("c", 8), ("ada_b", 48), ("norm_mix2", 8), ("mu", 7), ("w0", 2), ("a0", 2), ("kk", 2), ("ka", 2),
    ("rk", 2), ("lnw", 2), ("lnb", 2), ("sglw", 2), ("sglb", 2), ("cw", 6), ("s_are", 8), ("s_aim", 8),
    ("s_ldt", 8), ("s_d", 2), ("norm_ffn2", 8), ("final_g", 8),
]
VOFF, NVEC = {}, 0
for _n, _c in VECS:
    VOFF[_n] = NVEC
    NVEC += _c

CONSTS = [
    ("ones", 128), ("blk", 128), ("ident", 128), ("su", 128), ("iu", 128),
    ("l0", 128), ("l0t", 128), ("l1", 128), ("l2", 128), ("l3", 128), ("l4", 128), ("l5", 128),
    ("smask", 256), ("iota", 256), ("sgm", 128), ("bmask", 8), ("cmask", 32),
]
COFF, NCONST = {}, 0
for _n, _c in CONSTS:
    COFF[_n] = NCONST
    NCONST += _c


CONSTS2 = [("dm", 384), ("invc", 1024)]


def const_arrays():
    c = {}
    i = np.arange(128)
    s, t = i[:, None], i[None, :]
    c["ident"] = np.eye(128)
    c["ones"] = np.ones((128, 128))
    c["blk"] = s // 64 == t // 64
    q, k = i[:, None], np.arange(256)[None, :]
    lo = np.where(k[:, :128] <= q, k[:, :128] - q, -1e34)
    hi = np.where(k <= q + 128, k - (q + 128), -1e34)
    c["dm"] = np.concatenate([lo, hi], 1)
    n = np.arange(1, 257)
    c["invc"] = np.tile(np.concatenate([1.0 / np.minimum(n, w) for w in (2, 4, 8, 16)]), (128, 1))
    same = s // 64 == t // 64
    c["su"] = same & (s < t)
    c["iu"] = same & (s <= t)
    for v in range(6):
        m = (s >> (v + 1) == t >> (v + 1)) & ((s >> v) % 2 == 0) & ((t >> v) % 2 == 1)
        c[f"l{v}"] = m
        if v == 0:
            c["l0t"] = m.T
    c["smask"] = np.tile(np.arange(256) % 64 != 0, (128, 1))
    c["iota"] = np.tile(np.arange(256), (128, 1))
    c["sgm"] = s <= t
    g = i // 16
    c["bmask"] = g[:, None] == np.arange(8)[None, :]
    st = np.zeros((128, 4, 8))
    for j in range(4):
        st[:, j] = (2 * j + i // 64)[:, None] == np.arange(8)[None, :]
    c["cmask"] = st.reshape(128, 32)
    return [np.concatenate([np.asarray(c[n], np.float32) for n, _ in names], 1) for names in (CONSTS, CONSTS2)]


class Queue:

    def __init__(self, sem):
        self.sem, self.n, self.ops, self.seen = sem, 0, [], {}

    def wait(self, *toks):
        for tok in toks:
            if tok is None:
                continue
            if isinstance(tok, list):
                self.wait(*tok)
                continue
            sem, v = tok
            if self.seen.get(id(sem), 0) < v:
                self.seen[id(sem)] = v
                self.ops.append(lambda e, sem=sem, v=v: e.wait_ge(sem, v))

    def quiet(self, f, *toks):
        self.wait(*toks)
        self.ops.append(f)

    def run(self, f, *toks):
        self.wait(*toks)
        self.n += 1
        self.ops.append(lambda e: f(e).then_inc(self.sem, 1))
        return (self.sem, self.n)

    def dma(self, out, in_, sem, *toks):
        self.wait(*toks)
        self.ops.append(lambda e: e.dma_start(out, in_).then_inc(sem, 16))

    def play(self, e):
        for op in self.ops:
            op(e)


def split8(nk):
    n = -(-nk // 8)
    return [nk // n + (i < nk % n) for i in range(n)]


ADA_IN = ((), (2, 5, 8, 11, 14, 17, 20))
ADA_OUT = ((), (2,))
ADA_PA = (3, 4, 5, 6, 7, 8, 9)
ADA_RG = ((5, 7, 9), (1, 3, 5, 7, 8))
FILLS = "02222222111111111111111111111111111111"
YW = ((0, 2), (2, 2), (4, 2), (6, 4))


def weight_order():
    o = []

    def whole(w, nk, ms):
        for m in ms:
            k = 0
            for n in split8(nk):
                o.append((w, m, k, n))
                k += n

    ada = iter(range(24))

    def columns():
        n = next(ada)
        o.extend(("ada_w", n, z, 0) for z in range(2))

    whole("pa_w_in", 8, range(4, 16))
    for i in range(11):
        if 1 <= i < 5:
            whole("pa_w_in", 8, (i - 1,))
        if i in ADA_PA:
            columns()
    for m in range(8):
        whole("pa_w_out", 8, (m,))
        if m == 1:
            columns()
    for l in range(2):
        for m in range(22):
            whole(f"ffn_w_in{l}", 8, (m, m + 22))
            if m in ADA_IN[l]:
                columns()
        for m in range(8):
            whole(f"ffn_w_out{l}", 22, (m,))
            if m in ADA_OUT[l]:
                columns()
        if l == 0:
            for n in range(2):
                for m in range(10):
                    whole("rg_w_in", 8, (m + 10 - 10 * n,))
                    if m in ADA_RG[n]:
                        columns()
            o.extend(("rg_w_out", 0, k, 8) for k in range(10))
    for m in MIX_ORDER:
        if m < 100:
            whole("w_in", 8, (m,))
        else:
            o.append(("yw", m // 10 - 10, *YW[m % 10]))
    whole("w_o", 8, range(8))
    whole("ffn_w1", 8, range(32))
    whole("ffn_w2", 32, range(8))
    return o


MIX_ORDER = [
    11, 12, 13, 14, 15, 16, 7, 8, 9, 10, 17, 18, 27, 101, 28, 111, 29, 121, 30, 131,
    31, 141, 32, 151, 33, 161, 34, 171, 35, 102, 36, 112, 37, 122, 6, 2, 3, 0, 1, 4,
    5, 38, 132, 39, 142, 40, 152, 41, 162, 42, 172, 43, 103, 44, 113, 45, 123, 46, 133, 47,
    143, 48, 153, 49, 163, 50, 173, 19, 20, 21, 22, 23, 24, 25, 26, 100, 110, 120, 130, 140,
    150, 160, 170,
]


def build(nc, d, out, dbg=None):
    with ExitStack() as ctx:
        cnt = [0]

        def alloc(stack, name, shape, dt=F32):
            cnt[0] += 1
            return stack.enter_context(nc.sbuf_tensor(f"{name}_{cnt[0]}", shape, dt))

        def sem(name):
            return ctx.enter_context(nc.semaphore(name))

        PE, V, A, G, SP = (Queue(sem(n)) for n in ("s_pe", "s_dve", "s_act", "s_pool", "s_sp"))
        ps = [ctx.enter_context(nc.psum_tensor(f"ps{i}", [128, 512], F32)) for i in range(8)]

        free = [None] * 8
        held = [False] * 8
        turn = [0]

        def bank():
            b = turn[0] % 8
            while held[b]:
                turn[0] += 1
                b = turn[0] % 8
            turn[0] += 1
            held[b] = True
            PE.wait(free[b])
            return b, ps[b]

        def done(b, tok):
            held[b] = False
            free[b] = tok

        cst = alloc(ctx, "cst", [128, NCONST])
        vec = alloc(ctx, "vec", [128, NVEC])
        s_c = sem("s_c")
        s_par = sem("s_par")
        x = alloc(ctx, "x", [128, 8, T])
        hh = alloc(ctx, "hh", [128, 8, T], F32R)
        hl = alloc(ctx, "hl", [128, 8, T], F32R)
        raw = [alloc(ctx, f"raw{i}", [128, T]) for i in range(4)]
        s_x = sem("s_x")
        s_xm = [s_x] + [sem(f"s_x{m}") for m in range(1, 8)]
        for m in range(8):
            SP.dma(x[:, m, :], d["xT"][:, m, :], s_xm[m])
        A.dma(vec[:, :], d["vec"], s_c)
        A.dma(cst[:, 0:384], d["cst"][:, 0:384], s_c)
        s_c2 = sem("s_c2")
        t_c = (s_c, 32)

        def C(name, lo=0, hi=None):
            n = dict(CONSTS)[name]
            return cst[:, COFF[name] + lo:COFF[name] + (n if hi is None else hi)]

        def P(name, i=0, n=1):
            return vec[:, VOFF[name] + i:VOFF[name] + i + n]

        NR, NS, AHEAD = 6, 5, 3
        ring = [alloc(ctx, f"ring{i}", [128, 8, 128]) for i in range(NR)]
        whi = [alloc(ctx, f"whi{i}", [128, 8, 128], F32R) for i in range(NS)]
        wlo = [alloc(ctx, f"wlo{i}", [128, 8, 128], F32R) for i in range(NS)]
        rsem = [sem(f"s_ring{i}") for i in range(NR)]
        rfree = {}
        sfree = {}
        order = weight_order()
        nload, nuse = [0], [0]
        ready = {}

        def fetch():
            while nload[0] < len(order) and (nload[0] < NR or nload[0] - NR in rfree):
                n = nload[0]
                w, m, k, nk = order[n]
                i = n % NR
                if w == "rg_w_out":
                    src, dst = d[w][k], ring[i][:, :, :].rearrange("p a b -> p (a b)")
                elif w == "ada_w":
                    r, c = (m % 8) * 128, (m // 8) * 2048 + k * 1024
                    src, dst = d[w][r:r + 128, c:c + 1024], ring[i][:, :, :].rearrange("p a b -> p (a b)")
                else:
                    src, dst = d[w][m, :, k:k + nk, :], ring[i][:, 0:nk, :]
                SP.dma(dst, src, rsem[i], rfree.pop(n - NR, None))
                nload[0] += 1

        nhigh, nhalf, pend = [0], [0], []

        def highs(upto):
            while nhigh[0] < min(upto, len(order)):
                n = nhigh[0]
                w, m, k, nk = order[n]
                i = n % NR
                if nload[0] <= n:
                    return
                tok = (rsem[i], 16 * (n // NR + 1))
                if w == "ada_w":
                    ready[n] = (i, tok, None)
                else:
                    c = nhalf[0]
                    if c >= NS and c - NS not in sfree:
                        return
                    nhalf[0] += 1
                    t = act(whi[c % NS][:, 0:nk, :], ring[i][:, 0:nk, :], ACT.Copy, tok, sfree.pop(c - NS, None))
                    pend.append((n, c, nk, t))
                nhigh[0] += 1

        def prepare(upto):
            highs(upto)
            while pend and pend[0][0] < upto:
                n, c, nk, t = pend.pop(0)
                r, j = ring[n % NR][:, 0:nk, :], c % NS
                t = tt(wlo[j][:, 0:nk, :], r, whi[j][:, 0:nk, :].bitcast(F32), SUB, t)
                rfree[n] = t
                fetch()
                ready[n] = (j, t, c)
                highs(upto)
            highs(upto + 1)

        def load(*key):
            n = nuse[0]
            assert order[n] == key, (order[n], key)
            nuse[0] += 1
            prepare(n + 1)
            return ready.pop(n)

        def linear(w, ms, rhs, nk, outs, toks, each=None):
            k = 0
            assert nk <= 8 or len(ms) == 1
            for n in split8(nk):
                js = []
                for m in ms:
                    js.append(load(w, m, k, n))
                PE.wait(*toks)
                for q in range(n):
                    if each is not None:
                        PE.wait(each(k + q))
                    rh, rl = rhs(k + q)
                    for (j, tok, _), o in zip(js, outs):
                        PE.wait(tok)
                        a, b = k + q == 0, k + q == nk - 1
                        mm(o, whi[j][:, q, :], rh, start=a, stop=False, last=False)
                        mm(o, whi[j][:, q, :], rl, start=False, stop=False, last=False)
                        t = mm(o, wlo[j][:, q, :], rh, start=False, stop=b, last=q == n - 1)
                for _, _, c in js:
                    sfree[c] = t
                prepare(nuse[0] + AHEAD)
                k += n
            return t

        def split(hi, lo, src, t, w=None):
            t = act(hi, src, ACT.Copy, t, w)
            return tt(lo, src, hi.bitcast(F32), SUB, t)

        def mm(o, l, r, *toks, start=True, stop=True, last=True):
            f = lambda e: e.matmul(o, l, r, start=start, stop=stop)
            return PE.run(f, *toks) if last else PE.quiet(f, *toks)

        def act(o, i, func, *toks, scale=1.0, bias=0.0, acc=None):
            return A.run(lambda e: e.activation(o, i, func, bias=bias, scale=scale, accum_out=acc), *toks)

        def tt(o, a, b, op, *toks, q=None):
            return (q or V).run(lambda e: e.tensor_tensor(o, a, b, op), *toks)

        def ts(o, a, s1, s2, op0, op1, *toks, q=None):
            if s2 is None:
                return (q or V).run(lambda e: e.tensor_scalar(o, a, s1, None, op0), *toks)
            return (q or V).run(lambda e: e.tensor_scalar(o, a, s1, s2, op0, op1), *toks)

        def stt(o, a, s, b, op0, op1, *toks):
            return V.run(lambda e: e.scalar_tensor_tensor(out=o, in0=a, scalar=s, in1=b, op0=op0, op1=op1), *toks)

        def copy(o, i, *toks, q=None):
            q = q or V
            if q is A:
                return act(o, i, ACT.Copy, *toks)
            return q.run(lambda e: e.tensor_copy(o, i), *toks)

        def recip(o, i, *toks):
            return V.run(lambda e: e.reciprocal(o, i), *toks)

        MUL, ADD, SUB, MAX, MIN = ALU.mult, ALU.add, ALU.subtract, ALU.max, ALU.min
        ones, blk, ident = C("ones"), C("blk"), C("ident")

        rst = alloc(ctx, "rst", [128, T])
        sqa = alloc(ctx, "sqa", [128, T])
        sqt = alloc(ctx, "sqt", [128, 3, T])
        dmy = alloc(ctx, "dmy", [128, 1])
        t_dmy = [None]
        h_free = [None]
        raw_tok = [None] * 4
        t_acc = [None] * 9
        t_st = [None]

        def gather(m, t, q=G):
            if m == 0:
                t_acc[0] = act(sqa[:, :], x[:, 0, :], ACT.Square, t, t_st[0])
                return
            i = 2 if m == 7 else m % 2
            t = act(sqt[:, i, :], x[:, m, :], ACT.Square, t, t_acc[m - 2] if 2 < m < 7 else t_st[0])
            t_acc[m] = tt(sqa[:, :], sqa[:, :], sqt[:, i, :], ADD, t, t_acc[m - 1], q=q) if m < 7 else t
            if m == 5 and q is G:
                t_dmy[0] = act(dmy[:, :], C("ones", 0, 1), ACT.Sqrt, t_dmy[0])

        def norm_stats():
            b, p = bank()
            mm(p[:, 0:T], ones, sqa[:, :], t_acc[6], stop=False, last=False)
            t = mm(p[:, 0:T], ones, sqt[:, 2, :], t_acc[7], start=False)
            t_st[0] = t
            t = ts(rst[:, :], p[:, 0:T], 1.0 / 1024, 1e-6, MUL, ADD, t)
            done(b, t)
            t = act(rst[:, :], rst[:, :], ACT.Sqrt, t)
            return recip(rst[:, :], rst[:, :], t)

        def h_tiles(make):
            toks, t = [], [None] * 8
            for k in range(10):
                if k < 8:
                    t[k] = make(k, raw[k % 4][:, :])
                    t[k] = act(hh[:, k, :], raw[k % 4][:, :], ACT.Copy, t[k], h_free[0])
                if k >= 2:
                    q = k - 2
                    raw_tok[q % 4] = tt(hl[:, q, :], raw[q % 4][:, :], hh[:, q, :].bitcast(F32), SUB, t[q])
                    toks.append(raw_tok[q % 4])
            return toks

        def norm(gain):
            if nuse[0]:
                prepare(nuse[0] + 3)
            t = norm_stats()
            if not nuse[0]:
                prepare(3)
            return h_tiles(lambda k, r: stt(r, x[:, k, :], P(gain, k), rst[:, :], MUL, MUL, t, raw_tok[k % 4]))

        def residual(w, nk, rhs, each, scale=None, also=None):
            for ms in ([0, 1], [2], [3], [4], [5], [6], [7]) if nk == 8 else [[m] for m in range(8)]:
                got = [bank() for _ in ms]
                t = linear(w, ms, rhs, nk, [p[:, 0:T] for _, p in got], [], each=each)
                for m, (b, p) in zip(ms, got):
                    add_to_x(m, b, p, t, scale)
                    if also:
                        also(m)

        def add_to_x(m, b, p, t, scale=None, q=G):
            if scale is None:
                t = tt(x[:, m, :], p[:, 0:T], x[:, m, :], ADD, t)
            else:
                t = stt(x[:, m, :], p[:, 0:T], scale(m), x[:, m, :], MUL, ADD, t)
            done(b, t)
            gather(m, t, q)

        def residual_by_rows(w, nk, rhs, each, ahead):
            got = [bank() for _ in range(8)]
            for k in range(nk):
                j, tok, c = load(w, 0, k, 8)
                ahead(k)
                PE.wait(tok, each(k))
                rh, rl = rhs(k)
                for m, (b, p) in enumerate(got):
                    o, a, z = p[:, 0:T], whi[j][:, m, :], wlo[j][:, m, :]
                    mm(o, a, rh, start=k == 0, stop=False, last=False)
                    mm(o, a, rl, start=False, stop=False, last=False)
                    t = mm(o, z, rh, start=False, stop=k == nk - 1, last=m == 7 or k == nk - 1)
                    if k == nk - 1:
                        add_to_x(m, b, p, t, q=V)
                sfree[c] = t
                prepare(nuse[0] + AHEAD)

        def hk(k):
            return hh[:, k, :], hl[:, k, :]

        def parts(a, b):
            return lambda k: (a[:, k, :], b[:, k, :])

        def project(w, items, t_h):
            res = []
            at = 0
            while at < len(items):
                n = 3 if at == 0 and t_h[0] is not None and len(items) >= 3 else 1
                got = [bank() for _ in range(n)]
                t = linear(w, [items[at + i][0] for i in range(n)], hk, 8, [p[:, 0:T] for _, p in got], [],
                           each=lambda k: t_h[k])
                for i in range(n):
                    t1 = items[at + i][1](got[i][1][:, 0:T], t)
                    done(got[i][0], t1)
                    res.append(t1)
                at += n
            return res

        dbgs = []

        def dump(name, ap, tok):
            if dbg is not None and name in dbg:
                s = sem("dbg_" + name)
                A.dma(dbg[name], ap, s, tok)
                dbgs.append((s, 16))
                for q in (V, PE, A, G):
                    q.wait((s, 16))

        def pool_attn():
            t_h = norm("norm_mix0")
            with ExitStack() as st:
                u = alloc(st, "u", [128, 4, 16 + T])
                qk = alloc(st, "qk", [128, 8, T])
                sq = alloc(st, "sq", [128, 4, T])
                rq = alloc(st, "rq", [128, 2, T])
                vf = alloc(st, "vf", [128, 4, T])
                vt = alloc(st, "vt", [128, 2, 512])
                pa = alloc(st, "pa", [128, 8, T])
                pah = alloc(st, "pah", [128, 8, T], F32R)
                pal = alloc(st, "pal", [128, 8, T], F32R)
                ta = alloc(st, "ta", [128, 16 + T])
                tb = alloc(st, "tb", [128, 16 + T])
                pw = alloc(st, "pw", [128, 4, 128])
                gq = alloc(st, "gq", [128, 1])
                cst2 = alloc(st, "cst2", [128, 1408])
                A.dma(cst2[:, :], d["cst2"], s_par)
                A.dma(pw[:, :, :], d["pool_w"], s_par)
                A.dma(cst[:, 384:], d["cst"][:, 384:], s_c2)
                t_pw = (s_par, 32)
                V.run(lambda e: e.memset(u[:, :, 0:16], 0.0))
                V.run(lambda e: e.memset(ta[:, 0:16], 0.0))
                t0 = V.run(lambda e: e.memset(tb[:, 0:16], 0.0))
                t_g = ts(gq[:, :], P("q_gain"), 0.125, None, MUL, None)
                t_qk = [None] * 8
                t_sq = [None] * 8

                def head_norm(i, b, p):
                    b2, p2 = bank()
                    t2 = mm(p2[:, 0:T], blk, sq[:, i % 4, :], t_sq[i])
                    r = rq[:, i % 2, :]
                    t = ts(r, p2[:, 0:T], 1.0 / 64, 1e-6, MUL, ADD, t2, t_qk[i - 2] if i > 1 else None)
                    done(b2, t)
                    t = act(r, r, ACT.Sqrt, t)
                    t = recip(r, r, t)
                    t = stt(qk[:, i, :], p[:, 0:T], gq[:, :] if i < 4 else P("k_gain"), r, MUL, MUL, t, t_g)
                    done(b, t)
                    t_qk[i] = t

                at = []
                for ms in ([4, 5], [6], [7], [8], [9], [10], [11]):
                    got = [bank() for _ in ms]
                    t = linear("pa_w_in", ms, hk, 8, [p[:, 0:T] for _, p in got], [], each=lambda k: t_h[k])
                    for m, (b, p) in zip(ms, got):
                        i = m - 4
                        t_sq[i] = act(sq[:, i % 4, :], p[:, 0:T], ACT.Square, t, t_qk[i - 4] if i > 3 else None)
                        at.append((i, b, p))
                    while len(at) > 1:
                        head_norm(*at.pop(0))
                tv = []
                for m in range(12, 16):
                    b, p = bank()
                    t = linear("pa_w_in", [m], hk, 8, [p[:, 0:T]], [])
                    if at:
                        head_norm(*at.pop(0))
                    t = copy(vf[:, m - 12, :], p[:, 0:T], t, q=A)
                    done(b, t)
                    tv.append(t)
                t_v = []

                def values():
                    for z in range(2):
                        b, p = bank()
                        for j in range(4):
                            t = PE.run(lambda e, p=p, z=z, j=j: e.transpose(
                                p[:, j * 128:j * 128 + 128], vf[:, j, z * 128:z * 128 + 128], ident), tv)
                        t = copy(vt[:, z, :], p[:, :], t, q=A)
                        done(b, t)
                        t_v.append(t)

                prev = [t0]
                t_p = [None] * 4

                def pool(g):
                    b, p = bank()
                    t = linear("pa_w_in", [g], hk, 8, [p[:, 0:T]], [])
                    t = copy(u[:, g, 16:], p[:, 0:T], t, q=A)
                    done(b, t)
                    cur = u[:, g, :]
                    w_ = prev[0]
                    for w in range(g + 1):
                        s = 1 << w
                        nxt = (ta, tb)[w % 2]
                        t = tt(nxt[:, 16:], cur[:, 16:], cur[:, 16 - s:16 + T - s], ADD, t, w_)
                        cur = nxt
                    t = tt(cur[:, 16:], cur[:, 16:], cst2[:, 384 + g * T:384 + (g + 1) * T], MUL, t, t_pw)
                    t = tt(vf[:, g, :], cur[:, 16:], u[:, g, 16:], SUB, t, t_v)
                    prev[0] = t
                    t_p[g] = t

                def pool_out(g):
                    b, p = bank()
                    t = mm(p[:, 0:T], pw[:, g, :], vf[:, g, :], t_p[g], t_pw)
                    t = act(pa[:, g, :], p[:, 0:T], ACT.Copy, t, scale=P("pool_scale", g))
                    done(b, t)
                    t_p[g] = split(pah[:, g, :], pal[:, g, :], pa[:, g, :], t)

                L = alloc(st, "L", [128, 3, 384])
                PT = alloc(st, "PT", [128, 3, 384])
                sm = alloc(st, "sm", [128, 3, 8])
                t_a = [None] * 4
                t_L, t_T, t_PT, t_PV = ([None] * 11 for _ in range(4))

                def scores(hd):
                    j, r, z = hd // 2, 64 * (hd % 2), hd % 3
                    b, p = bank()
                    qh, kh = qk[r:r + 64, j, :], qk[r:r + 64, 4 + j, :]
                    mm(p[:, 0:128], qh[:, 0:128], kh[:, 0:128], t_qk[7], last=False)
                    t = mm(p[:, 128:384], qh[:, 128:256], kh)
                    slope = 2.0 ** (-8.0 * (hd + 1) / 8)
                    t = stt(L[:, z, :], cst2[:, 0:384], slope, p[:, 0:384], MUL, ADD, t, t_pw, t_T[hd - 3] if hd > 2 else None)
                    done(b, t)
                    s = sm[:, z, :]
                    V.run(lambda e: e.tensor_reduce(s[:, 0:1], L[:, z, 0:128], AX, MAX, negate=True), t)
                    t = V.run(lambda e: e.tensor_reduce(s[:, 1:2], L[:, z, 128:384], AX, MAX, negate=True), t)
                    act(L[:, z, 0:128], L[:, z, 0:128], ACT.Exp, t, bias=s[:, 0:1], acc=s[:, 2:3])
                    t = act(L[:, z, 128:384], L[:, z, 128:384], ACT.Exp, bias=s[:, 1:2], acc=s[:, 3:4])
                    t = recip(s[:, 4:6], s[:, 2:4], t)
                    ts(L[:, z, 0:128], L[:, z, 0:128], s[:, 4:5], None, MUL, None, t)
                    t_L[hd] = ts(L[:, z, 128:384], L[:, z, 128:384], s[:, 5:6], None, MUL, None)

                def turn_p(hd):
                    z = hd % 3
                    b, p = bank()
                    for n in range(3):
                        t = PE.run(lambda e, n=n: e.transpose(
                            p[:, n * 128:(n + 1) * 128], L[:, z, n * 128:(n + 1) * 128], ident), t_L[hd])
                    t_T[hd] = t
                    t_PT[hd] = copy(PT[:, z, :], p[:, 0:384], t, t_PV[hd - 3] if hd > 2 else None, q=A)
                    done(b, t_PT[hd])

                def values_of(hd):
                    j, r, z = hd // 2, 64 * (hd % 2), hd % 3
                    b, p = bank()
                    o = p[r:r + 64, :]
                    mm(o[:, 0:256], vt[:, 0, hd * 64:hd * 64 + 64], PT[:, z, 0:256], t_PT[hd], t_v, last=False, stop=False)
                    t = mm(o[:, 128:256], vt[:, 1, hd * 64:hd * 64 + 64], PT[:, z, 256:384], start=False)
                    t_PV[hd] = t
                    t = copy(pa[r:r + 64, 4 + j, :], o[:, 0:256], t)
                    done(b, t)
                    return split(pah[r:r + 64, 4 + j, :], pal[r:r + 64, 4 + j, :], pa[r:r + 64, 4 + j, :], t)

                for i in range(11):
                    if i == 1:
                        values()
                    if i < 8:
                        scores(i)
                    if 1 <= i < 5:
                        pool(i - 1)
                    if 1 <= i < 9:
                        turn_p(i - 1)
                    if 2 <= i < 6:
                        pool_out(i - 2)
                    if 2 <= i < 10:
                        t_a[(i - 2) // 2] = values_of(i - 2)
                    if i in ADA_PA:
                        mod_step()
                h_free[0] = (PE.sem, PE.n)
                dump("pa", pa[:, :, :], t_a)

                def also(m):
                    next(steps, None)
                    mod_turn()
                    if m == 0:
                        mod_step()

                residual("pa_w_out", 8, parts(pah, pal), lambda k: t_p[k] if k < 4 else t_a[k - 4], also=also)

        def conv_taps(z, src, wname, nm, m, taps, t, bias):
            t = act(z, src, ACT.Identity, t, scale=P(wname, (taps - 1) * nm + m), bias=bias)
            for s in range(1, taps):
                t = stt(z[:, s:], src[:, 0:T - s], P(wname, (taps - 1 - s) * nm + m), z[:, s:], MUL, ADD, t)
            return t

        def conv_ffn(l):
            t_h = norm(f"norm_ffn{l}")
            with ExitStack() as st:
                hidh = alloc(st, "hidh", [128, 22, T], F32R)
                hidl = alloc(st, "hidl", [128, 22, T], F32R)
                zu = alloc(st, "zu", [128, 3, T])
                zg = alloc(st, "zg", [128, 3, T])
                V.wait(t_st[0])
                A.wait(t_st[0])
                old = [None] * 3

                def use_u(m):
                    return lambda p, t: conv_taps(zu[:, m % 3, :], p, f"ffn_cw{l}", 44, m, 3, [t, old[m % 3]], P(f"ffn_cb{l}", m))

                def use_g(m):
                    def use(p, t):
                        z = zg[:, m % 3, :]
                        t = conv_taps(z, p, f"ffn_cw{l}", 44, m + 22, 3, [t, old[m % 3]], P(f"ffn_cb{l}", m + 22))
                        t_z[m] = t
                        return t
                    return use

                t_z, t_h2, t_hid = {}, {}, {}

                def behind(m):
                    if m >= 2:
                        k = m - 2
                        z = zg[:, k % 3, :]
                        old[k % 3] = t_hid[k] = split(hidh[:, k, :], hidl[:, k, :], z, t_h2[k])
                    if 1 <= m <= 22:
                        k = m - 1
                        z = zg[:, k % 3, :]
                        t = act(z, z, ACT.Gelu_apprx_tanh, t_z[k])
                        t_h2[k] = tt(z, z, zu[:, k % 3, :], MUL, t)

                w = f"ffn_w_in{l}"
                for m in range(0, 22):
                    if m == 0:
                        got = [bank(), bank()]
                        t = linear(w, [0, 22], hk, 8, [p[:, 0:T] for _, p in got], [], each=lambda k: t_h[k])
                        for (b, p), use in zip(got, (use_u(0), use_g(0))):
                            done(b, use(p[:, 0:T], t))
                    else:
                        for c, use in ((m, use_u(m)), (m + 22, use_g(m))):
                            b, p = bank()
                            t = linear(w, [c], hk, 8, [p[:, 0:T]], [])
                            done(b, use(p[:, 0:T], t))
                    behind(m)
                    if m in ADA_IN[l]:
                        mod_step()
                behind(22)
                behind(23)
                h_free[0] = (PE.sem, PE.n)

                def also(m):
                    if l == 0:
                        next(steps, None)
                        next(steps, None)
                    mod_turn()
                    if m in ADA_OUT[l]:
                        mod_step()

                residual(f"ffn_w_out{l}", 22, parts(hidh, hidl), lambda k: t_hid[k], also=also)

        def rglru():
            t_h = norm("norm_mix1")
            with ExitStack() as st:
                gate = alloc(st, "gate", [128, 10, T])
                xr = alloc(st, "xr", [128, 10, T])
                rr = alloc(st, "rr", [128, 10, T])
                ii = alloc(st, "ii", [128, 10, T])
                yh = alloc(st, "yh", [128, 10, T], F32R)
                yl = alloc(st, "yl", [128, 10, T], F32R)
                wab = alloc(st, "wab", [128, 20, 128])
                cf = alloc(st, "cf", [128, 8, 10])
                sc = alloc(st, "sc", [128, 2, T])
                V.wait(t_st[0])
                A.wait(t_st[0])
                s_w = sem("s_wab")
                A.dma(wab[:, :, :], d["rg_wab"], s_w)
                t_w = (s_w, 16)
                lam = P("rg_lam", 0, 10)
                c = [cf[:, n, :] for n in range(8)]

                def decay():
                    t = ts(c[0], lam, -1.0, 0.0, MUL, MAX)
                    t = ts(c[1], lam, -1.0, None, MUL, None)
                    t = tt(c[1], c[1], lam, MIN, t)
                    t = act(c[1], c[1], ACT.Exp, t)
                    t = ts(c[2], c[1], 2.0, None, ADD, None, t)
                    t = recip(c[2], c[2], t)
                    t = tt(c[1], c[1], c[2], MUL, t)
                    t = tt(c[2], c[1], c[1], MUL, t)
                    t = ts(c[3], c[2], 1.0 / 17, 1.0 / 15, MUL, ADD, t)
                    for n in (13, 11, 9, 7, 5, 3, 1):
                        t = tt(c[3], c[3], c[2], MUL, t)
                        t = ts(c[3], c[3], 1.0 / n, None, ADD, None, t)
                    t = tt(c[3], c[3], c[1], MUL, t)
                    t = stt(c[3], c[3], 2.0, c[0], MUL, ADD, t)
                    ts(c[4], c[3], -8.0, None, MUL, None, t)
                    return ts(c[5], c[3], 8.0, None, MUL, None, t)

                tx, tr = [None] * 10, [None] * 10

                def use_x(m):
                    def use(p, t):
                        tx[m] = conv_taps(xr[:, m, :], p, "rg_cw", 10, m, 4, t, P("rg_cb", m))
                        return tx[m]
                    return use

                def ri(m):
                    b, p = bank()
                    b2, p2 = bank()
                    t = mm(p[:, 0:T], wab[:, m, :], xr[:, m, :], tx[m], t_w)
                    t2 = mm(p2[:, 0:T], wab[:, 10 + m, :], xr[:, m, :])
                    t = act(rr[:, m, :], p[:, 0:T], ACT.Sigmoid, t, bias=P("rg_ba", m))
                    done(b, t)
                    t = act(ii[:, m, :], p2[:, 0:T], ACT.Sigmoid, t2, bias=P("rg_bx", m))
                    done(b2, t)
                    tr[m] = tt(ii[:, m, :], ii[:, m, :], xr[:, m, :], MUL, t, q=G)

                got = [bank() for _ in range(3)]
                t = linear("rg_w_in", [10, 11, 12], hk, 8, [p[:, 0:T] for _, p in got], [], each=lambda k: t_h[k])
                for m, (b, p) in enumerate(got):
                    done(b, use_x(m)(p[:, 0:T], t))
                t_cf = decay()
                tg = [None] * 10
                t_sc = [None, None]
                ty = [None] * 10

                def gate_of(m):
                    b, p = bank()
                    t = linear("rg_w_in", [m], hk, 8, [p[:, 0:T]], [])
                    tg[m] = copy(gate[:, m, :], p[:, 0:T], t, q=A)
                    done(b, tg[m])

                th, tq = {}, {}

                def decays(ms):
                    for m in ms:
                        t = act(xr[:, m, :], rr[:, m, :], ACT.Tanh, tr[m], t_cf, scale=c[5][:, m:m + 1])
                        t = act(rr[:, m, :], rr[:, m, :], ACT.Exp, t, scale=c[4][:, m:m + 1])
                        th[m] = t

                def sizes(ms):
                    for m in ms:
                        s = sc[:, m % 2, :]
                        t = ts(s, xr[:, m, :], 1.0, None, ADD, None, th[m], t_sc[m % 2])
                        t = recip(s, s, t)
                        t = stt(xr[:, m, :], xr[:, m, :], 2.0, s, MUL, MUL, t)
                        t_sc[m % 2] = tq[m] = t

                def roots(ms):
                    for m in ms:
                        tq[m] = act(xr[:, m, :], xr[:, m, :], ACT.Sqrt, tq[m])

                def scans(ms):
                    for m in ms:
                        t = act(gate[:, m, :], gate[:, m, :], ACT.Gelu_apprx_tanh, tg[m])
                        t2 = tt(ii[:, m, :], ii[:, m, :], xr[:, m, :], MUL, tq[m])
                        t2 = V.run(lambda e, m=m: e.tensor_tensor_scan(xr[:, m, :], rr[:, m, :], ii[:, m, :], 0.0, MUL, ADD), t2)
                        t = tt(gate[:, m, :], gate[:, m, :], xr[:, m, :], MUL, t, t2)
                        ty[m] = split(yh[:, m, :], yl[:, m, :], gate[:, m, :], t)

                for m in range(3, 10):
                    b, p = bank()
                    t = linear("rg_w_in", [m + 10], hk, 8, [p[:, 0:T]], [])
                    done(b, use_x(m)(p[:, 0:T], t))
                    if m == 3:
                        ri(0)
                        ri(1)
                    ri(m - 1)
                    if m in ADA_RG[0]:
                        mod_step()
                for m in range(10):
                    gate_of(m)
                    mod_turn()
                    if m in ADA_RG[1]:
                        mod_step()
                    if m == 0:
                        ri(9)
                    if m in (3, 5, 7, 9):
                        roots({3: (0, 1, 2), 5: (3, 4, 5), 7: (6, 7), 9: (8, 9)}[m])
                    sizes(((), (0, 1), (2,), (3, 4), (5,), (6,), (7,), (8,), (9,), ())[m])
                    if m in (0, 2, 4, 6):
                        decays({0: (0, 1, 2), 2: (3, 4, 5), 4: (6, 7), 6: (8, 9)}[m])
                    if m >= 7:
                        scans((m - 7,))
                h_free[0] = (PE.sem, PE.n)
                scans((3,))
                residual_by_rows("rg_w_out", 10, parts(yh, yl), lambda k: ty[k],
                                 ahead=lambda k: scans(range(4 + k, min(10, 5 + k))))

        cosT = alloc(ctx, "cosT", [128, 8, T])
        sinT = alloc(ctx, "sinT", [128, 8, T])
        s5p = alloc(ctx, "s5p", [128, 20, 8])
        mod = alloc(ctx, "mod", [128, 48])
        gsc = alloc(ctx, "gsc", [128, 2, 8])
        sc32 = alloc(ctx, "sc32", [128, 8, 32])
        mrow = alloc(ctx, "mrow", [128, 512])

        def round_off(a, tmp, t):
            t = ts(tmp, a, ROUND, ROUND, ADD, SUB, t)
            return tt(a, a, tmp, SUB, t)

        def s5_params(w, tmp):
            c = [s5p[:, n, :] for n in range(20)]
            dt, lr, mag, ph, qre, qim = c[0], c[1], c[2], c[3], c[4], c[5]
            t = act(dt, P("s_ldt", 0, 8), ACT.Exp)
            t = ts(lr, P("s_are", 0, 8), -1e-4, None, MIN, None, t)
            t = tt(mag, lr, dt, MUL, t)
            t = act(mag, mag, ACT.Exp, t)
            yield
            t = tt(c[6], P("s_aim", 0, 8), dt, MUL, t)
            t = ts(c[7], c[6], 1.0 / TWO_PI, None, MUL, None, t)
            t = ts(c[7], c[7], ROUND, ROUND, ADD, SUB, t)
            c1 = 6.28125
            c2 = float(np.float32(0.0019340515136718750))
            c3 = TWO_PI - c1 - c2
            for v in (c1, c2, c3):
                t = stt(c[6], c[7], -v, c[6], MUL, ADD, t)
            t = ts(ph, c[6], 1.0 / TWO_PI, None, MUL, None, t)
            yield
            t = round_off(ph, c[7], t)
            t = ts(c[8], ph, 0.25, None, ADD, None, t)
            t = round_off(c[8], c[7], t)
            t = act(c[8], c[8], ACT.Sin, t, scale=6.283185)
            t = act(c[9], ph, ACT.Sin, t, scale=6.283185)
            yield
            t = tt(c[8], c[8], mag, MUL, t)
            t = ts(c[8], c[8], 1.0, None, SUB, None, t)
            t = tt(c[9], c[9], mag, MUL, t)
            li = P("s_aim", 0, 8)
            t = tt(c[10], lr, lr, MUL, t)
            t = tt(c[11], li, li, MUL, t)
            t = tt(c[10], c[10], c[11], ADD, t)
            t = recip(c[10], c[10], t)
            yield
            t = tt(c[11], c[8], lr, MUL, t)
            t = tt(c[12], c[9], li, MUL, t)
            t = tt(c[11], c[11], c[12], ADD, t)
            t = tt(qre, c[11], c[10], MUL, t)
            yield
            t = tt(c[11], c[9], lr, MUL, t)
            t = tt(c[12], c[8], li, MUL, t)
            t = tt(c[11], c[11], c[12], SUB, t)
            t = tt(qim, c[11], c[10], MUL, t)
            yield
            big = ROUND / 4096.0
            t = ts(c[13], ph, big, big, ADD, SUB, t)
            t_ph = tt(c[14], ph, c[13], SUB, t)
            V.wait((s_c2, 16))
            yield
            yield
            t_s = [None, None]
            for n in range(8):
                a, e = w[:, 2 * (n % 2), :], w[:, 2 * (n % 2) + 1, :]
                t = ts(a, C("iota"), c[13][:, n:n + 1], None, MUL, None, t_ph, t_s[n % 2])
                t = round_off(a, tmp[:, :], t)
                t = stt(a, C("iota"), c[14][:, n:n + 1], a, MUL, ADD, t)
                t = round_off(a, tmp[:, :], t)
                yield
                t1 = ts(e, a, 0.25, None, ADD, None, t)
                t1 = round_off(e, tmp[:, :], t1)
                act(sinT[:, n, :], a, ACT.Sin, t, scale=6.283185)
                t_s[n % 2] = act(cosT[:, n, :], e, ACT.Sin, t1, scale=6.283185)
                yield
            V.wait(t_s)

        mst = {"n": 0}

        def mod_start():
            sc = s5p[:, 15, :]
            t = act(sc, P("c", 0, 8), ACT.Sigmoid)
            t = tt(sc, sc, P("c", 0, 8), MUL, t)
            mst["t"] = copy(sc32[:, :, :], sc.unsqueeze(2).to_broadcast([128, 8, 32]), t)

        def mod_step():
            n = mst["n"]
            mst["n"] += 1
            r, k = n // 8, n % 8
            if k == 0:
                mst["b"] = bank()
            b, p = mst["b"]
            for z in range(2):
                i, tok, _ = load("ada_w", n, z, 0)
                for y in range(2):
                    g = 2 * z + y
                    t = mm(p[32 * g:32 * g + 32, :], sc32[:, k, :],
                           ring[i][:, 4 * y:4 * y + 4, :], tok, mst["t"], start=k == 0, stop=k == 7)
                rfree[nuse[0] - 1] = t
                fetch()
            prepare(nuse[0] + AHEAD)
            if k == 7:
                t = copy(mrow[:, :], p[:, :], t, mst.get("x"), q=A)
                done(b, t)
                mst["late"] = (r, t)

        def mod_turn():
            if "late" in mst:
                r, t = mst.pop("late")
                b, p = bank()
                for q in range(4):
                    t1 = PE.run(lambda e, q=q, p=p: e.transpose(p[:, q * 128:q * 128 + 128], mrow[:, q * 128:q * 128 + 128], ident), t)
                mst["x"] = t1
                o = mod[:, 16 * r:16 * r + 16].rearrange("p (g q) -> p g q", q=4)
                a_ = P("ada_b", 16 * r, 16).rearrange("p (g q) -> p g q", q=4)
                i_ = p[:, :].rearrange("p (q g s) -> p g q s", g=4, s=32)[:, :, :, 0]
                mst["t_m"] = tt(o, i_, a_, ADD, t1)
                done(b, mst["t_m"])

        def mod_end():
            for n, nm in enumerate(("norm_mix2", "norm_ffn2")):
                t = stt(gsc[:, n, :], mod[:, 24 * n + 8:24 * n + 16], 1.0, P(nm, 0, 8), ADD, MUL, mst["t_m"])
            return t

        def mod_norm(n, t_m):
            prepare(nuse[0] + 3)
            t = norm_stats()

            def make(k, r):
                t1 = tt(r, x[:, k, :], rst[:, :], MUL, t, raw_tok[k % 4])
                return act(r, r, ACT.Identity, t1, t_m, scale=gsc[:, n, k:k + 1], bias=mod[:, 24 * n + k:24 * n + k + 1])

            return h_tiles(make)

        def mixers(t_m):
            t_h = mod_norm(0, t_m)
            with ExitStack() as st:
                ga = alloc(st, "ga", [128, 8, T])
                pm = alloc(st, "pm", [128, 8, T])
                gt = alloc(st, "gt", [128, 3, T])
                yinh = alloc(st, "yinh", [128, 8, T], F32R)
                yinl = alloc(st, "yinl", [128, 8, T], F32R)
                lora = alloc(st, "lora", [128, 256])
                s_l = sem("s_lora")
                for q in (V, A, G):
                    q.wait(t_st[0], (s_c2, 16))
                A.dma(lora[:, :], d["lora"], s_l)
                t_l = (s_l, 16)

                def proj(m, use):
                    b, p = bank()
                    t = linear("w_in", [m], hk, 8, [p[:, 0:T]], [], each=lambda k: t_h[k])
                    t = use(p[:, 0:T], t)
                    done(b, t)
                    return t

                def rwkv():
                    s2 = ExitStack()
                    al = lambda n, sh: alloc(s2, n, sh)
                    f = {n: al(n, [128, 2, T]) for n in ("r", "k", "v", "b", "ks", "at", "rt", "bn", "g", "e")}
                    lo = al("lo", [128, T])
                    omu = al("omu", [128, 8])
                    t_o = ts(omu[:, 0:7], P("mu", 0, 7), -1.0, 1.0, MUL, ADD)
                    t_o = ts(omu[:, 7:8], P("mu", 0, 1), 0.0, None, MUL, None)

                    def shift(o, m):
                        def use(p, t):
                            t = act(o, p, ACT.Copy, t, t_o, scale=omu[:, m:m + 1])
                            return stt(o[:, 1:], p[:, 0:T - 1], P("mu", m), o[:, 1:], MUL, ADD, t)
                        return proj(m, use)

                    t_lo = shift(lo[:, :], 6)
                    tk = [shift(f["k"][:, j, :], 2 + j) for j in range(2)]
                    tr = [shift(f["r"][:, j, :], j) for j in range(2)]
                    tv = [shift(f["v"][:, j, :], 4 + j) for j in range(2)]
                    yield
                    t1 = act(lo[0:32, :], lo[0:32, :], ACT.Tanh, t_lo)
                    t2 = act(lo[64:128, :], lo[64:128, :], ACT.Sigmoid, t_lo)
                    ld, e = al("ld", [128, 2, T]), f["e"]
                    aa = al("aa", [128, 2, T])
                    b, p = bank()
                    b2, p2 = bank()
                    b3, p3 = bank()
                    for j in range(2):
                        c, o = slice(j * 128, j * 128 + 128), slice(j * T, j * T + T)
                        ta = mm(p[:, o], lora[0:32, c], lo[0:32, :], t1, t2, t_l)
                        tb = mm(p2[:, o], lora[32:64, c], lo[32:64, :])
                        tc = mm(p3[:, o], lora[64:128, c], lo[64:128, :])
                    for j in range(2):
                        o = slice(j * T, j * T + T)
                        ta = act(ld[:, j, :], p[:, o], ACT.Sigmoid, tc, bias=P("w0", j))
                        tb = act(aa[:, j, :], p2[:, o], ACT.Sigmoid, bias=P("a0", j))
                    for j in range(2):
                        tc = copy(f["g"][:, j, :], p3[:, j * T:j * T + T], q=A)
                    done(b, ta)
                    done(b2, tb)
                    done(b3, tc)
                    yield
                    t_ld = ts(ld[:, :, :], ld[:, :, :], -0.6065306597126334, None, MUL, None, ta)
                    cs, mid, en = al("cs", [128, 2, T]), al("mid", [128, 8]), al("en", [128, 8])
                    for j in range(2):
                        t = V.run(lambda e_, j=j: e_.tensor_tensor_scan(cs[:, j, :], C("smask"), ld[:, j, :], 0.0, MUL, ADD), t_ld)
                    c4 = cs[:, :, :].rearrange("p j (c t) -> p (j c) t", t=64)
                    t = copy(mid[:, :].unsqueeze(2), c4[:, :, 31:32], t)
                    t = tt(c4, c4, mid[:, :].unsqueeze(2).to_broadcast([128, 8, 64]), SUB, t)
                    t_c = t
                    t = copy(en[:, :].unsqueeze(2), c4[:, :, 63:64], t)
                    m4, e4 = mid[:, :].rearrange("p (j c) -> p j c", j=2), en[:, :].rearrange("p (j c) -> p j c", j=2)
                    t = tt(e4[:, :, 0:3], e4[:, :, 0:3], m4[:, :, 1:4], ADD, t)
                    t_f = act(en[:, :], en[:, :], ACT.Exp, t)
                    t = tt(ld[:, :, :], cs[:, :, :], ld[:, :, :], SUB, t_c)
                    t_e1 = act(f["rt"][:, :, :], cs[:, :, :], ACT.Exp, t_c)
                    t_e2 = act(cs[:, :, :], cs[:, :, :], ACT.Exp, t_e1, t, scale=-1.0)
                    t_e3 = act(ld[:, :, :], ld[:, :, :], ACT.Exp, t)
                    yield
                    kh, b_ = f["at"], f["b"]
                    for j in range(2):
                        t = ts(kh[:, j, :], f["k"][:, j, :], P("kk", j), None, MUL, None, tk[j])
                    t = tt(e[:, :, :], kh[:, :, :], kh[:, :, :], MUL, t)
                    yield
                    b, p = bank()
                    t = mm(p[:, 0:512], blk, e[:, :, :], t)
                    t = act(e[:, :, :], p[:, 0:512].rearrange("p (j t) -> p j t", j=2), ACT.Sqrt, t)
                    done(b, t)
                    t = ts(e[:, :, :], e[:, :, :], 1e-12, None, MAX, None, t)
                    t = recip(e[:, :, :], e[:, :, :], t)
                    t = tt(kh[:, :, :], kh[:, :, :], e[:, :, :], MUL, t)
                    t = tt(b_[:, :, :], kh[:, :, :], aa[:, :, :], MUL, t, tb)
                    for j in range(2):
                        t1 = ts(aa[:, j, :], aa[:, j, :], 1.0, P("ka", j), SUB, MUL, t)
                    t1 = stt(f["k"][:, :, :], aa[:, :, :], 1.0, f["k"][:, :, :], ADD, MUL, t1)
                    for j in range(2):
                        t2 = stt(e[:, j, :], f["r"][:, j, :], P("rk", j), f["k"][:, j, :], MUL, MUL, t1, tr[j])
                    yield
                    b, p = bank()
                    t2 = mm(p[:, 0:512], blk, e[:, :, :], t2)
                    t_bn = tt(f["bn"][:, :, :], p[:, 0:512].rearrange("p (j t) -> p j t", j=2), f["v"][:, :, :], MUL, t2, tv)
                    done(b, t_bn)
                    t = stt(kh[:, :, :], kh[:, :, :], -1.0, ld[:, :, :], MUL, MUL, t_e3, t)
                    t = tt(f["rt"][:, :, :], f["rt"][:, :, :], f["r"][:, :, :], MUL, t_e1)
                    t = tt(b_[:, :, :], b_[:, :, :], cs[:, :, :], MUL, t_e2)
                    t_s = tt(f["ks"][:, :, :], f["k"][:, :, :], cs[:, :, :], MUL, t_e2)
                    At, Rt, Bs, Ks = f["at"], f["rt"], f["b"], f["ks"]
                    BT, (KT, VT) = cs, (al(n, [128, 2, 256]) for n in ("KT", "VT"))
                    t_tr = {}
                    yield
                    for nm, src, dst in (("b", Bs, BT), ("k", Ks, KT), ("v", f["v"], VT)):
                        b, p = bank()
                        for z in range(2):
                            for j in range(2):
                                t = PE.run(lambda e_, p=p, z=z, j=j, src=src: e_.transpose(
                                    p[:, (2 * z + j) * 128:(2 * z + j + 1) * 128],
                                    src[:, j, z * 128:(z + 1) * 128], ident), t_s, tv)
                        t = copy(dst[:, :, :], p[:, 0:512].rearrange("p (z c) -> p z c", z=2), t, q=A)
                        done(b, t)
                        t_tr[nm] = t
                    yield
                    N, NR_, MK = (al(n, [128, 2, 4, 128]) for n in ("N", "NR", "MK"))
                    MR = [mrow[:, :].rearrange("p (h t) -> p h t", h=4),
                          sqt[:, 0:2, :].rearrange("p a t -> p (a t)").rearrange("p (h t) -> p h t", h=4)]
                    v4 = lambda a, i: a[:, 4 * i:4 * i + 4, :].rearrange("p a t -> p (a t)").rearrange(
                        "p (z h t) -> p z h t", z=2, h=4)
                    X, Y, Q, NL = v4(cosT, 0), v4(cosT, 1), v4(sinT, 0), v4(sinT, 1)

                    def bc(name):
                        return C(name).unsqueeze(1).to_broadcast([128, 4, 128])

                    tn, tmk, tnr, t_xy = [None] * 2, [None] * 2, [None] * 2, [None] * 2
                    for z in range(2):
                        zs = slice(z * 128, z * 128 + 128)
                        for dst, l, r, mk in ((N, Bs, At, "su"), (NR_, Bs, Rt, "iu"), (MK, Ks, At, "su"), (None, Ks, Rt, "iu"), (NL, At, Bs, "l0t")):
                            b, p = bank()
                            for hd in (0, 2, 1, 3):
                                j, r0 = hd // 2, 64 * (hd % 2)
                                t = mm(p[:, hd * 128:hd * 128 + 128], l[r0:r0 + 64, j, zs], r[r0:r0 + 64, j, zs],
                                       t if hd == 1 else t_s)
                            o = MR[z] if dst is None else dst[:, z, :, :]
                            t = tt(o, p[:, :].rearrange("p (h t) -> p h t", h=4), bc(mk), MUL, t)
                            done(b, t)
                        t = tt(Y[:, z, :, :], NL[:, z, :, :], bc("ident"), ADD, t)
                        t2 = tt(X[:, z, :, :], N[:, z, :, :], bc("l0"), MUL, t)
                        t_xy[z] = tt(X[:, z, :, :], X[:, z, :, :], bc("ident"), ADD, t2)
                        yield
                    for lv in range(1, 6):
                        for z in range(2):
                            t = tt(NL[:, z, :, :], N[:, z, :, :], bc(f"l{lv}"), MUL, t_xy[z])
                            b, p = bank()
                            for hd in range(4):
                                t1 = mm(p[:, hd * 128:hd * 128 + 128], NL[:, z, hd, :], Y[:, z, hd, :], t)
                            t1 = copy(Q[:, z, :, :], p[:, :].rearrange("p (h t) -> p h t", h=4), t1, q=A)
                            done(b, t1)
                            t_xy[z] = t1
                        yield
                        for z in range(2):
                            t1 = t_xy[z]
                            b, p = bank()
                            for hd in range(4):
                                t2 = mm(p[:, hd * 128:hd * 128 + 128], Q[:, z, hd, :], X[:, z, hd, :], t1)
                            if lv < 5:
                                b3, p3 = bank()
                                for hd in range(4):
                                    t2 = mm(p3[:, hd * 128:hd * 128 + 128], X[:, z, hd, :], Q[:, z, hd, :])
                            t = tt(X[:, z, :, :], p[:, :].rearrange("p (h t) -> p h t", h=4), X[:, z, :, :], ADD, t2)
                            done(b, t)
                            if lv < 5:
                                t = tt(Y[:, z, :, :], p3[:, :].rearrange("p (h t) -> p h t", h=4), Y[:, z, :, :], ADD, t2)
                                done(b3, t)
                            t_xy[z] = t
                        yield
                    U0, SA, R = f["r"], ld, aa
                    S0 = [r[:, :].rearrange("p (j i) -> p j i", j=2) for r in raw]
                    for z in range(2):
                        b, p = bank()
                        for hd in range(4):
                            t = mm(p[:, hd * 64:hd * 64 + 64], MK[:, z, hd, :], VT[:, z, hd * 64:hd * 64 + 64], t_xy[z], t_tr["v"])
                        t = copy(U0[:, z, :], p[:, 0:256], t, q=A)
                        done(b, t)
                    t_u = t
                    t_s0 = V.run(lambda e_: e_.memset(S0[0], 0.0))
                    yield
                    for c in range(4):
                        z, q0 = c // 2, 64 * (c % 2)
                        rows = slice(q0, q0 + 64)
                        b, p = bank()
                        for j in range(2):
                            t = mm(p[:, j * 128:j * 128 + 128], At[:, j, z * 128:z * 128 + 128], S0[c][:, j, :], t_s0)
                        t = tt(R[rows, z, :], p[rows, 0:256], U0[rows, z, :], ADD, t, t_u)
                        done(b, t)
                        yield
                        b, p = bank()
                        for hd in range(4):
                            t2 = mm(p[rows, hd * 64:hd * 64 + 64], X[rows, z, hd, rows], R[rows, z, hd * 64:hd * 64 + 64], t)
                        t_sa = copy(SA[rows, z, :], p[rows, 0:256], t2, q=A)
                        done(b, t_sa)
                        if c == 3:
                            break
                        yield
                        b, p = bank()
                        for j in range(2):
                            js = slice(j * 128, j * 128 + 128)
                            mm(p[:, js], KT[rows, z, js], VT[rows, z, js], t_tr["k"], t_tr["b"], stop=False, last=False)
                            t = mm(p[:, js], BT[rows, z, js], SA[rows, z, js], t_sa, start=False)
                        nx = S0[c + 1]
                        t = tt(nx, p[:, 0:256].rearrange("p (j i) -> p j i", j=2), C("blk").unsqueeze(1).to_broadcast([128, 2, 128]), MUL, t)
                        done(b, t)
                        t = tt(nx, nx, S0[c], ADD, t)
                        for j in range(2):
                            t_s0 = ts(S0[c + 1][:, j, :], S0[c + 1][:, j, :], en[:, 4 * j + c:4 * j + c + 1], None, MUL, None, t, t_f)
                        yield
                    o_ = f["k"]
                    for j in range(2):
                        b, p = bank()
                        for u in range(2):
                            hd, r0 = 2 * j + u, 64 * u
                            for z in range(2):
                                o = p[r0:r0 + 64, z * 128:z * 128 + 128]
                                mm(o, SA[:, z, hd * 64:hd * 64 + 64], NR_[:, z, hd, :], t_sa, last=False, stop=False)
                                mm(o, VT[:, z, hd * 64:hd * 64 + 64], MR[z][:, hd, :], last=False, stop=False, start=False)
                                for y in range(2):
                                    c = 2 * z + y
                                    t = mm(p[r0:r0 + 64, c * 64:c * 64 + 64], S0[c][:, j, r0:r0 + 64], Rt[:, j, c * 64:c * 64 + 64],
                                           t_s0, start=False, stop=y == 1)
                        t = copy(o_[:, j, :], p[:, 0:T], t, q=A)
                        done(b, t)
                    dump("o", o_[:, :, :], t)
                    yield
                    b, p = bank()
                    t1 = mm(p[:, :], blk, o_[:, :, :], t)
                    yield
                    p_ = p[:, :].rearrange("p (j t) -> p j t", j=2)
                    t = stt(o_[:, :, :], p_, -1.0 / 64, o_[:, :, :], MUL, ADD, t1)
                    done(b, t)
                    t1 = tt(e[:, :, :], o_[:, :, :], o_[:, :, :], MUL, t)
                    b, p = bank()
                    t1 = mm(p[:, :], blk, e[:, :, :], t1)
                    yield
                    p_ = p[:, :].rearrange("p (j t) -> p j t", j=2)
                    t1 = ts(e[:, :, :], p_, 1.0 / 64, 64e-5, MUL, ADD, t1)
                    done(b, t1)
                    t1 = act(e[:, :, :], e[:, :, :], ACT.Sqrt, t1)
                    t1 = recip(e[:, :, :], e[:, :, :], t1)
                    for j in range(2):
                        t = stt(o_[:, j, :], o_[:, j, :], P("lnw", j), e[:, j, :], MUL, MUL, t1)
                        t = stt(o_[:, j, :], o_[:, j, :], P("lnb", j), f["bn"][:, j, :], ADD, ADD, t)
                    t = tt(o_[:, :, :], o_[:, :, :], f["g"][:, :, :], MUL, t)
                    dump("ya", o_[:, :, :], t)
                    toks["a"] = split(yinh[:, 0:2, :], yinl[:, 0:2, :], o_[:, :, :], t)
                    s2.close()

                def s5():
                    s2 = ExitStack()
                    al = lambda n, sh: alloc(s2, n, sh)
                    u = al("su", [128, 2, T])
                    bd = al("bd", [128, 2, 2, 64])
                    bp = al("bp", [128, 2, 2, 8, 64])
                    cd = al("cd", [128, 2, 8, 16])
                    cc = al("cc", [128, 2, 8, 16])
                    cp = al("cp", [128, 2, 8, 128])
                    s_b = sem("s_s5")
                    gate_ = (V.sem, V.n)
                    A.dma(bd[:, :, :, :], d["s5b"], s_b, gate_, (PE.sem, PE.n), (G.sem, G.n))
                    A.dma(cd[:, :, :, :], d["s5c"], s_b)
                    t_b = (s_b, 32)
                    tu = [proj(17 + j, lambda p, t, j=j: copy(u[:, j, :], p, t, q=A)) for j in range(2)]
                    yield
                    bm = C("bmask").unsqueeze(2).to_broadcast([128, 8, 64])
                    for ri in range(2):
                        for hf in range(2):
                            t = tt(bp[:, ri, hf, :, :], bd[:, ri, hf, :].unsqueeze(1).to_broadcast([128, 8, 64]), bm, MUL, t_b)
                    t_bp = t
                    qre = s5p[:, 4, :].unsqueeze(2).to_broadcast([128, 8, 16])
                    qim = s5p[:, 5, :].unsqueeze(2).to_broadcast([128, 8, 16])
                    cr, ci = cd[:, 0, :, :], cd[:, 1, :, :]
                    t = tt(cc[:, 0, :, :], cr, qre, MUL, t_b)
                    t1 = tt(cc[:, 1, :, :], ci, qim, MUL, t_b)
                    t = tt(cc[:, 0, :, :], cc[:, 0, :, :], cc[:, 1, :, :], SUB, t, t1)
                    t1 = tt(cc[:, 1, :, :], cr, qim, MUL, t)
                    t2 = tt(cd[:, 0, :, :], ci, qre, MUL, t1)
                    t1 = stt(cc[:, 1, :, :], cc[:, 1, :, :], -1.0, cd[:, 0, :, :], MUL, SUB, t1, t2)
                    cm = C("cmask").rearrange("p (j g) -> p j g", j=4)
                    for ri in range(2):
                        for i in range(8):
                            m = cm[:, i % 4, :].unsqueeze(2).to_broadcast([128, 8, 16])
                            s = cc[:, ri, i, :].unsqueeze(1).to_broadcast([128, 8, 16])
                            t = tt(cp[:, ri, i, :].rearrange("p (g c) -> p g c", g=8), s, m, MUL, t, t1)
                    t_cp = t
                    yield
                    z = al("z", [128, 2, 8, T])
                    w = al("sw", [128, 4, T])
                    old = [None, None]
                    for i in range(8):
                        hf = i // 4
                        co, si = cosT[:, i, :], sinT[:, i, :]
                        b, p = bank()
                        b2, p2 = bank()
                        t = mm(p[:, 0:T], bp[:, 0, hf, 2 * (i % 4):2 * (i % 4) + 2, :], u[:, hf, :], t_bp, tu[hf])
                        t2 = mm(p2[:, 0:T], bp[:, 1, hf, 2 * (i % 4):2 * (i % 4) + 2, :], u[:, hf, :])
                        w_ = [w[:, n, :] if i % 2 else raw[n][:, :] for n in range(4)]
                        ta = tt(w_[0], p[:, 0:T], co, MUL, t, old[i % 2])
                        tb = tt(w_[3], p[:, 0:T], si, MUL, t)
                        done(b, tb)
                        tc = tt(w_[1], p2[:, 0:T], si, MUL, t2)
                        td = tt(w_[2], p2[:, 0:T], co, MUL, t2)
                        done(b2, td)
                        ta = tt(w_[0], w_[0], w_[1], ADD, tc)
                        tb = tt(w_[2], w_[2], w_[3], SUB, td)
                        mg = s5p[:, 2, i:i + 1].to_broadcast([128, T])
                        ta = V.run(lambda e, w_=w_, mg=mg: e.tensor_tensor_scan(w_[1], mg, w_[0], 0.0, MUL, ADD), ta)
                        tb = V.run(lambda e, w_=w_, mg=mg: e.tensor_tensor_scan(w_[3], mg, w_[2], 0.0, MUL, ADD), tb)
                        ta = tt(w_[0], w_[1], co, MUL, ta, tb, q=G)
                        tb = tt(w_[2], w_[3], si, MUL, tb, q=G)
                        tc = tt(w_[3], w_[3], co, MUL, tb, q=G)
                        td = tt(w_[1], w_[1], si, MUL, ta, q=G)
                        ta = tt(z[:, 0, i, :], w_[0], w_[2], SUB, ta, tb, q=G)
                        tb = tt(z[:, 1, i, :], w_[3], w_[1], ADD, tc, td, q=G)
                        old[i % 2] = tb
                        yield
                    yield
                    for hf in range(2):
                        b, p = bank()
                        n = 0
                        for i in range(4 * hf, 4 * hf + 4):
                            for ri in range(2):
                                t = mm(p[:, 0:T], cp[:, ri, i, :], z[:, ri, i, :], t_cp, tb, start=n == 0, stop=n == 7)
                                n += 1
                        t = stt(u[:, hf, :], u[:, hf, :], P("s_d", hf), p[:, 0:T], MUL, ADD, t)
                        done(b, t)
                        t = act(u[:, hf, :], u[:, hf, :], ACT.Gelu_apprx_tanh, t)
                    dump("yd", u[:, :, :], t)
                    toks["d"] = split(yinh[:, 6:8, :], yinl[:, 6:8, :], u[:, :, :], t)
                    s2.close()

                def sg():
                    s2 = ExitStack()
                    al = lambda n, sh: alloc(s2, n, sh)
                    gu = al("gu", [128, 2, T])
                    gv = al("gv", [128, 2, T])
                    e = al("ge", [128, 2, T])
                    me = al("me", [128, T])
                    ws = al("ws", [128, 4, 128])
                    bs_ = al("bs", [128, 2, 128])
                    vT = al("gvT", [128, 2, 256])
                    s_g = sem("s_sg")
                    A.dma(ws[:, :, :], d["sg_ws"], s_g, (V.sem, V.n), (PE.sem, PE.n), (G.sem, G.n))
                    A.dma(bs_[:, :, :], d["sg_bs"], s_g)
                    tu = [proj(7 + j, lambda p, t, j=j: act(gu[:, j, :], p, ACT.Gelu_apprx_tanh, t)) for j in range(2)]
                    tv = [proj(9 + j, lambda p, t, j=j: act(gv[:, j, :], p, ACT.Gelu_apprx_tanh, t)) for j in range(2)]
                    yield
                    t_w = tt(ws[:, :, :], ws[:, :, :], C("sgm").unsqueeze(1).to_broadcast([128, 4, 128]), MUL, (s_g, 32))
                    b, p = bank()
                    for j in range(2):
                        t = mm(p[:, 0:T], ones, gv[:, j, :], tv[j], start=j == 0, stop=j == 1)
                    t = ts(me[:, :], p[:, 0:T], 1.0 / 256, None, MUL, None, t)
                    done(b, t)
                    t = tt(gv[:, :, :], gv[:, :, :], me[:, :].unsqueeze(1).to_broadcast([128, 2, T]), SUB, t)
                    t1 = tt(e[:, :, :], gv[:, :, :], gv[:, :, :], MUL, t)
                    yield
                    b, p = bank()
                    for j in range(2):
                        t = mm(p[:, 0:T], ones, e[:, j, :], t1, start=j == 0, stop=j == 1)
                    t = ts(me[:, :], p[:, 0:T], 1.0 / 256, 1e-5, MUL, ADD, t)
                    done(b, t)
                    t = act(me[:, :], me[:, :], ACT.Sqrt, t)
                    t = recip(me[:, :], me[:, :], t)
                    for j in range(2):
                        t1 = stt(gv[:, j, :], gv[:, j, :], P("sglw", j), me[:, :], MUL, MUL, t)
                        t1 = ts(gv[:, j, :], gv[:, j, :], P("sglb", j), None, ADD, None, t1)
                    yield
                    b, p = bank()
                    for z in range(2):
                        for j in range(2):
                            t = PE.run(lambda e_, p=p, z=z, j=j: e_.transpose(
                                p[:, (2 * z + j) * 128:(2 * z + j + 1) * 128], gv[:, j, z * 128:z * 128 + 128], ident), t1)
                    t = copy(vT[:, :, :], p[:, :].rearrange("p (z c) -> p z c", z=2), t, q=A)
                    done(b, t)
                    yield
                    for j in range(2):
                        b, p = bank()
                        for u in range(2):
                            g = 2 * j + u
                            for z in range(2):
                                t1 = mm(p[64 * u:64 * u + 64, z * 128:z * 128 + 128], vT[:, z, g * 64:g * 64 + 64], ws[:, g, :], t, t_w)
                        t1 = tt(e[:, j, :].rearrange("p (z t) -> p z t", z=2), p[:, 0:T].rearrange("p (z t) -> p z t", z=2),
                                bs_[:, j, :].unsqueeze(1).to_broadcast([128, 2, 128]), ADD, t1)
                        done(b, t1)
                    t = tt(e[:, :, :], e[:, :, :], gu[:, :, :], MUL, t1, tu[1])
                    dump("yb", e[:, :, :], t)
                    toks["b"] = split(yinh[:, 2:4, :], yinl[:, 2:4, :], e[:, :, :], t)
                    s2.close()

                def sconv():
                    s2 = ExitStack()
                    al = lambda n, sh: alloc(s2, n, sh)
                    c = {n: al("c" + n, [128, 2, T]) for n in ("b", "c", "y")}
                    V.wait((PE.sem, PE.n), (G.sem, G.n))
                    A.wait((V.sem, V.n), (PE.sem, PE.n), (G.sem, G.n))
                    tb = [proj(11 + j, lambda p, t, j=j: copy(c["b"][:, j, :], p, t, q=A)) for j in range(2)]
                    tc = [proj(13 + j, lambda p, t, j=j: copy(c["c"][:, j, :], p, t, q=A)) for j in range(2)]
                    for j in range(2):
                        ci = c["c"][:, j, :]
                        t = proj(15 + j, lambda p, t, ci=ci, j=j: tt(ci, p, ci, MUL, t, tc[j]))
                        t = conv_taps(c["y"][:, j, :], ci, "cw", 2, j, 3, t, 0.0)
                        t = tt(c["y"][:, j, :], c["y"][:, j, :], c["b"][:, j, :], MUL, t, tb[j])
                    dump("yc", c["y"][:, :, :], t)
                    toks["c"] = split(yinh[:, 4:6, :], yinl[:, 4:6, :], c["y"][:, :, :], t)
                    s2.close()
                    return
                    yield

                toks = {}
                t_ga, t_pm, t_gt = [None] * 8, [None] * 8, [None] * 3
                at = [0]

                def y_of(m, n, y, halves):
                    i, tok, c = load("yw", m, *YW[n])
                    b, p = bank()
                    PE.wait(tok, toks["abcd"[n]])
                    for v in range(halves):
                        o = p[:, v * T:v * T + T]
                        for k in range(2):
                            a, z, f, l = whi[i][:, 2 * v + k, :], wlo[i][:, 2 * v + k, :], yinh[:, y + k, :], yinl[:, y + k, :]
                            mm(o, a, f, start=k == 0, stop=False, last=False)
                            mm(o, a, l, start=False, stop=False, last=False)
                            t = mm(o, z, f, start=False, stop=k == 1)
                    sfree[c] = t
                    prepare(nuse[0] + AHEAD)
                    return b, p, t

                def merge(m, n):
                    if n == 0:
                        t_ga[m] = proj(19 + m, lambda p, t: act(ga[:, m, :], p, ACT.Sigmoid, t))
                        return
                    i = at[0] % 3
                    at[0] += 1
                    g = gt[:, i, :]
                    t_g = proj(19 + 8 * n + m, lambda p, t: act(g, p, ACT.Sigmoid, t, t_gt[i]))
                    b, p, t = y_of(m, n, 2 * n, 2 if n == 3 else 1)
                    if n == 3:
                        j = at[0] % 3
                        at[0] += 1
                        e = gt[:, j, :]
                        t = act(e, p[:, T:2 * T], ACT.Sigmoid, t, t_gt[j])
                        t_g = tt(g, g, e, MUL, t, t_g)
                        t_gt[j] = t_g
                    o = pm[:, m, :] if n == 1 else g
                    t = tt(o, p[:, 0:T], g, MUL, t, t_g)
                    done(b, t)
                    if n > 1:
                        t = tt(pm[:, m, :], pm[:, m, :], g, ADD, t, t_pm[m])
                    t_gt[i] = t_pm[m] = t

                fills = [(m, n) for n in (1, 2, 3, 0) for m in range(8)]
                for part, skip in ((sconv, 0), (sg, 9), (s5, 0), (rwkv, 0)):
                    for q in (V, A, G):
                        q.wait((PE.sem, PE.n), (V.sem, V.n), (A.sem, A.n), (G.sem, G.n))
                    for n, _ in enumerate(part()):
                        for _ in range(int(FILLS[n]) if part is rwkv else n >= skip):
                            if fills:
                                merge(*fills.pop(0))
                while fills:
                    merge(*fills.pop(0))
                mgh = alloc(st, "mgh", [128, 8, T], F32R)
                mgl = alloc(st, "mgl", [128, 8, T], F32R)
                for q in (V, A):
                    q.wait((PE.sem, PE.n), (V.sem, V.n), (A.sem, A.n), (G.sem, G.n))
                old = [None] * 8
                for m in range(8):
                    b, p, t = y_of(m, 0, 0, 1)
                    g = ga[:, m, :]
                    t = tt(g, p[:, 0:T], g, MUL, t, t_ga[m])
                    done(b, t)
                    t = tt(g, g, pm[:, m, :], ADD, t, t_pm[m])
                    old[m] = split(mgh[:, m, :], mgl[:, m, :], g, t)
                h_free[0] = (PE.sem, PE.n)
                residual("w_o", 8, parts(mgh, mgl), lambda k: old[k], scale=lambda m: mod[:, 16 + m:17 + m])

        def relu_ffn(t_m):
            t_h = mod_norm(1, t_m)
            with ExitStack() as st:
                hidh = alloc(st, "hidh2", [128, 32, T], F32R)
                hidl = alloc(st, "hidl2", [128, 32, T], F32R)
                z = alloc(st, "zz", [128, 4, T])
                for q in (V, A):
                    q.wait(t_st[0])
                old = [None] * 4
                tz, t_hid = [], {}

                def parts_of(m, t):
                    old[m % 4] = t_hid[m] = split(hidh[:, m, :], hidl[:, m, :], z[:, m % 4, :], t)

                def use(m):
                    def f(p, t):
                        r = z[:, m % 4, :]
                        t1 = act(r, p, ACT.Relu, t, old[m % 4])
                        tz.append((m, act(r, r, ACT.Square, t1)))
                        if len(tz) > 1:
                            parts_of(*tz.pop(0))
                        return t1
                    return f

                project("ffn_w1", [(m, use(m)) for m in range(32)], t_h)
                parts_of(*tz.pop(0))
                h_free[0] = (PE.sem, PE.n)
                residual("ffn_w2", 32, parts(hidh, hidl), lambda k: t_hid[k], scale=lambda m: mod[:, 40 + m:41 + m])

        fetch()
        for m in range(8):
            gather(m, (s_xm[m], 16), V)
        for q in (PE, V, A, G):
            q.wait(t_c)
        s5s = ExitStack()
        steps = s5_params(alloc(s5s, "w", [128, 4, T]), alloc(s5s, "tmp", [128, T]))
        mod_start()
        pool_attn()
        conv_ffn(0)
        for _ in steps:
            pass
        s5s.close()
        dump("x2", x[:, :, :], (V.sem, V.n))
        rglru()
        dump("x3", x[:, :, :], (V.sem, V.n))
        conv_ffn(1)
        dump("x4", x[:, :, :], (V.sem, V.n))
        t_m = mod_end()
        mixers(t_m)
        dump("x5", x[:, :, :], (V.sem, V.n))
        relu_ffn(t_m)
        dump("x6", x[:, :, :], (V.sem, V.n))
        t = norm_stats()
        for k in range(8):
            t_o = stt(x[:, k, :], x[:, k, :], P("final_g", k), rst[:, :], MUL, MUL, t)
        assert nuse[0] == len(order)
        s_out = sem("s_out")
        SP.dma(out, x[:, :, :], s_out, t_o)
        SP.wait((s_out, 16))
        SP.wait(*dbgs)

        with nc.Block() as block:
            @block.sync
            def _(e):
                SP.play(e)

            @block.scalar
            def _(e):
                A.play(e)

            @block.vector
            def _(e):
                V.play(e)

            @block.gpsimd
            def _(e):
                G.play(e)

            @block.tensor
            def _(e):
                PE.play(e)


def lay(i):
    a = {k: np.asarray(v) for k, v in i.items()}

    def tiles(w):
        k, m = w.shape
        return np.ascontiguousarray(w.reshape(k // 128, 128, m // 128, 128).transpose(2, 1, 0, 3))

    def cols(v):
        return v.reshape(-1, 128).T

    o = {}
    o["xT"] = a["x"][0].T.reshape(8, 128, 256).transpose(1, 0, 2)
    o["cst"], o["cst2"] = const_arrays()
    v = {
        "norm_mix0": a["norm_mix"][0], "norm_mix1": a["norm_mix"][1], "norm_ffn0": a["norm_ffn"][0],
        "norm_ffn1": a["norm_ffn"][1], "pool_scale": a["pa_pool_scale"][0],
        "q_gain": np.concatenate([a["pa_q_gain"][0]] * 2), "k_gain": np.concatenate([a["pa_k_gain"][0]] * 2),
        "rg_cw": a["rg_conv_w"][0], "rg_cb": a["rg_conv_b"][0], "rg_ba": a["rg_b_a"][0], "rg_bx": a["rg_b_x"][0],
        "rg_lam": a["rg_lambda"][0], "ffn_cw0": a["ffn_conv_w"][0], "ffn_cw1": a["ffn_conv_w"][1],
        "ffn_cb0": a["ffn_conv_b"][0], "ffn_cb1": a["ffn_conv_b"][1], "c": a["c_2"], "ada_b": a["ada_b_2"],
        "norm_mix2": a["norm_mix_g_2"], "mu": a["rwkv_mu_2"], "w0": a["rwkv_w0_2"], "a0": a["rwkv_a0_2"],
        "kk": a["rwkv_kk_2"], "ka": a["rwkv_ka_2"], "rk": a["rwkv_rk_2"], "lnw": a["rwkv_lnx_w_2"],
        "lnb": a["rwkv_lnx_b_2"], "sglw": a["sg_ln_w_2"], "sglb": a["sg_ln_b_2"], "cw": a["conv_w_2"],
        "s_are": a["s5_a_re_2"], "s_aim": a["s5_a_im_2"], "s_ldt": np.repeat(a["s5_log_dt_2"].reshape(16), 64),
        "s_d": a["s5_d_2"], "norm_ffn2": a["norm_ffn_g_2"], "final_g": a["final_g_2"],
    }
    o["vec"] = np.concatenate([cols(v[n]) for n, _ in VECS], 1)
    o["pa_w_in"] = tiles(a["pa_w_in"][0])
    o["pool_w"] = a["pa_pool_w"][0].transpose(1, 0, 2)
    o["pa_w_out"] = tiles(a["pa_w_out"][0])
    o["rg_w_in"] = tiles(a["rg_w_in"][0])
    o["rg_wab"] = np.concatenate([a["rg_w_a"][0], a["rg_w_x"][0]], 0).transpose(1, 0, 2)
    o["rg_w_out"] = a["rg_w_out"][0].reshape(10, 128, 1024)
    for l in range(2):
        o[f"ffn_w_in{l}"] = tiles(a["ffn_w_in"][l])
        o[f"ffn_w_out{l}"] = tiles(a["ffn_w_out"][l])
    o["ada_w"] = a["ada_w_2"][0]
    o["w_in"] = tiles(a["w_in_2"][0])
    o["lora"] = np.concatenate([a["rwkv_w2_2"][0], a["rwkv_a2_2"][0], a["rwkv_g2_2"][0]], 0)
    glu = tiles(a["s5_glu_w_2"][0])
    o["yw"] = np.concatenate([tiles(a["rwkv_out_2"][0]), tiles(a["sg_out_2"][0]), tiles(a["conv_out_2"][0]),
                              glu[:8], glu[8:]], 2)
    o["sg_ws"] = a["sg_ws_2"][0].transpose(2, 0, 1)
    o["sg_bs"] = np.repeat(a["sg_bs_2"][0], 64, 0).reshape(2, 128, 128).transpose(1, 0, 2)
    sb = np.stack([a["s5_b_re_2"][0], a["s5_b_im_2"][0]]).reshape(2, 2, 8, 64, 16)
    o["s5b"] = sb.transpose(2, 4, 0, 1, 3).reshape(128, 2, 2, 64)
    sc = np.stack([a["s5_c_re_2"][0], a["s5_c_im_2"][0]]).reshape(2, 8, 2, 16, 64)
    o["s5c"] = sc.transpose(2, 4, 0, 1, 3).reshape(128, 2, 8, 16)
    o["w_o"] = tiles(a["w_o_2"][0])
    o["ffn_w1"] = tiles(a["ffn_w1_2"][0])
    o["ffn_w2"] = tiles(a["ffn_w2_2"][0])
    return {k: np.ascontiguousarray(w) for k, w in o.items()}


def kernel(**inputs):
    import concourse.bacc as bacc
    from concourse.bass_utils import run_bass_kernel_spmd

    arrays = lay(inputs)
    nc = bacc.Bacc("TRN2", target_bir_lowering=False, num_devices=1)
    d = {n: nc.dram_tensor(n, a.shape, F32, kind="ExternalInput").ap() for n, a in arrays.items()}
    out = nc.dram_tensor("out", (128, 8, 256), F32, kind="ExternalOutput").ap()
    build(nc, d, out)
    r = run_bass_kernel_spmd(nc, [arrays], core_ids=[0])
    o = r.results[0]["out"]
    return o.transpose(1, 0, 2).reshape(1024, 256).T.reshape(1, 256, 1024)
```
